# Optimizing a Trainium2 kernel written in Bass

```python
import math
import jax, jax.numpy as jnp
from jax import lax
import numpy as np

D_MODEL = 2048
BATCH = 1
SEQ = 512
DEPTH = 1

CTX_LEN = 256
GRID_W = 64
EPS = 1e-6

MIX_W = D_MODEL
HY_W = D_MODEL // 4
MLA_HEADS = 8
MLA_DN = 128
MLA_DR = 64
MLA_DV = 128
MLA_W = MLA_HEADS * MLA_DV
Q_RANK = D_MODEL // 4
KV_RANK = D_MODEL // 8
POOL_W = D_MODEL // 4
POOL_WINDOWS = (2, 4, 8, 16)
N_POOL_GROUPS = len(POOL_WINDOWS)
POOL_GROUP = POOL_W // N_POOL_GROUPS

SHORT_CONV = 3
FILTER_EMB = 33
FILTER_BANDS = (FILTER_EMB - 1) // 2
FILTER_HIDDEN = 64
DECAY_TARGET = 1e-2
FAST_DECAY = 0.3
SLOW_DECAY = 1.5

ROPE_BASE = 10000.0
Q_BLOCK = 128
ATTN_SCALE = (MLA_DN + MLA_DR) ** -0.5

OFF_HY = 0
OFF_HY_G = OFF_HY + 3 * HY_W
OFF_Q = OFF_HY_G + HY_W
OFF_KV = OFF_Q + Q_RANK
OFF_KR = OFF_KV + KV_RANK
OFF_MLA_G = OFF_KR + MLA_DR
OFF_POOL = OFF_MLA_G + MLA_W
OFF_POOL_G = OFF_POOL + POOL_W
N_IN = OFF_POOL_G + POOL_W

kernel_name = "hybrid_hyena_mla_pool_prefix_dit"

def rmsnorm(x, g):
    xf = x.astype(jnp.float32)
    y = xf * lax.rsqrt(jnp.mean(xf * xf, axis=-1, keepdims=True) + EPS)
    return (y * g.astype(jnp.float32)).astype(x.dtype)

def adaln(cond, w_ada, b_ada):
    mod = jax.nn.silu(cond) @ w_ada + b_ada
    shift, scale, gate = jnp.split(mod[:, None, :], 3, axis=-1)
    return shift, scale, gate

def rope_tables(L):
    n_rows = L // GRID_W
    row = jnp.broadcast_to(jnp.arange(n_rows, dtype=jnp.float32)[:, None], (n_rows, GRID_W)).reshape(L)
    col = jnp.broadcast_to(jnp.arange(GRID_W, dtype=jnp.float32)[None, :], (n_rows, GRID_W)).reshape(L)
    n_freq = MLA_DR // 4
    inv = ROPE_BASE ** (-jnp.arange(n_freq, dtype=jnp.float32) / n_freq)
    ang = jnp.concatenate([row[:, None] * inv, col[:, None] * inv], axis=-1)
    return jnp.cos(ang), jnp.sin(ang)

def apply_rope(x, cos, sin):
    xf = x.astype(jnp.float32).reshape(*x.shape[:-1], -1, 2)
    x0, x1 = xf[..., 0], xf[..., 1]
    out = jnp.stack([x0 * cos - x1 * sin, x0 * sin + x1 * cos], axis=-1)
    return out.reshape(x.shape).astype(x.dtype)

def short_conv(u, w, b):
    L = u.shape[1]
    up = jnp.pad(u, ((0, 0), (1, 1), (0, 0)))
    return up[:, :L] * w[0] + up[:, 1:L + 1] * w[1] + up[:, 2:] * w[2] + b

def hyena_spectrum(L, w1, b1, freq, w2, b2, w3):
    f32 = jnp.float32
    t = jnp.linspace(0.0, 1.0, L, dtype=f32)[:, None]
    wpos = (2.0 * math.pi / L) * jnp.arange(L, dtype=f32)[:, None]
    bands = jnp.linspace(1e-4, FILTER_BANDS - 1, FILTER_BANDS, dtype=f32)[None, :]
    feats = jnp.concatenate([t, jnp.cos(bands * wpos), -jnp.sin(bands * wpos)], axis=-1)
    h = jnp.sin(freq * (feats @ w1 + b1))
    h = jnp.sin(freq * (h @ w2 + b2))
    h = (h @ w3).astype(f32).reshape(L, 2, 2, HY_W)
    deltas = jnp.abs(jnp.linspace(math.log(DECAY_TARGET) / SLOW_DECAY,
                                  math.log(DECAY_TARGET) / FAST_DECAY, HY_W, dtype=f32))
    h = h * jnp.exp(-t[:, :, None, None] * deltas)
    k = jnp.concatenate([h[:, :, 0], jnp.zeros_like(h[:1, :, 0]), h[:0:-1, :, 1]], axis=0)
    k = k * lax.rsqrt(jnp.sum(k * k, axis=0, keepdims=True) + EPS)
    return jnp.fft.rfft(k, axis=0)

def fft_long_conv(z, k_f, bias):
    L = z.shape[1]
    zf = z.astype(jnp.float32)
    y = jnp.fft.irfft(jnp.fft.rfft(zf, n=2 * L, axis=1) * k_f, n=2 * L, axis=1)[:, :L]
    return (y + zf * bias.astype(jnp.float32)).astype(z.dtype)

def hyena_mix(u, lp):
    L = u.shape[1]
    u = short_conv(u, lp["hy_conv_w"], lp["hy_conv_b"])
    v, x1, x2 = jnp.split(u, 3, axis=-1)
    k_f = hyena_spectrum(L, lp["hf_w1"], lp["hf_b1"], lp["hf_freq"], lp["hf_w2"], lp["hf_b2"], lp["hf_w3"])
    z = x1 * fft_long_conv(v, k_f[:, 0], lp["hy_bias"][0])
    return x2 * fft_long_conv(z, k_f[:, 1], lp["hy_bias"][1])

def mla_queries(u_q, q_norm_g, w_uq, rope):
    B, L, _ = u_q.shape
    q = (rmsnorm(u_q, q_norm_g) @ w_uq).reshape(B, L, MLA_HEADS, MLA_DN + MLA_DR)
    q_nope, q_rope = q[..., :MLA_DN], q[..., MLA_DN:]
    if rope is not None:
        q_rope = apply_rope(q_rope, rope[0][:, None, :], rope[1][:, None, :])
    return q_nope, q_rope

def mla_keys(u_kvr, kv_norm_g, w_ukv, rope):
    B, L, _ = u_kvr.shape
    kv = (rmsnorm(u_kvr[..., :KV_RANK], kv_norm_g) @ w_ukv).reshape(B, L, MLA_HEADS, MLA_DN + MLA_DV)
    k_rope = u_kvr[..., KV_RANK:]
    if rope is not None:
        k_rope = apply_rope(k_rope, rope[0], rope[1])
    return kv[..., :MLA_DN], k_rope, kv[..., MLA_DN:]

def attend(q_nope, q_rope, k_nope, k_rope, v):
    s = (jnp.einsum('bqhd,bkhd->bhqk', q_nope, k_nope)
         + jnp.einsum('bqhr,bkr->bhqk', q_rope, k_rope))
    p = jax.nn.softmax(s.astype(jnp.float32) * ATTN_SCALE, axis=-1).astype(v.dtype)
    return jnp.einsum('bhqk,bkhd->bqhd', p, v)

def blocked_attend(q_nope, q_rope, k_nope, k_rope, v):
    B, L, H, _ = q_nope.shape
    nb = L // Q_BLOCK
    qn = q_nope.reshape(B, nb, Q_BLOCK, H, MLA_DN).swapaxes(0, 1)
    qr = q_rope.reshape(B, nb, Q_BLOCK, H, MLA_DR).swapaxes(0, 1)
    o = lax.map(lambda qb: attend(qb[0], qb[1], k_nope, k_rope, v), (qn, qr))
    return o.swapaxes(0, 1).reshape(B, L, H * MLA_DV)

def pool_mix(u, w_pool, pool_scale):
    B, L, _ = u.shape
    uf = u.astype(jnp.float32).reshape(B, L, N_POOL_GROUPS, POOL_GROUP)
    cs = jnp.pad(jnp.cumsum(uf, axis=1), ((0, 0), (1, 0), (0, 0), (0, 0)))
    t = jnp.arange(L)[:, None]
    halves = jnp.asarray(np.array([w // 2 for w in POOL_WINDOWS], dtype=np.int32))[None, :]
    lo = jnp.clip(t - halves, 0, L)
    hi = jnp.clip(t + halves, 0, L)
    gid = jnp.arange(N_POOL_GROUPS)[None, :]
    mean = (cs[:, hi, gid] - cs[:, lo, gid]) / (hi - lo).astype(jnp.float32)[None, :, :, None]
    d = (mean - uf).astype(u.dtype)
    y = jnp.einsum('blgc,gcd->blgd', d, w_pool).reshape(B, L, POOL_W)
    return y * pool_scale

def mixer(u, keys, lp, rope, blocked):
    B, L, _ = u.shape
    hy = hyena_mix(u[..., OFF_HY:OFF_HY_G], lp) * jax.nn.silu(u[..., OFF_HY_G:OFF_Q])
    q_nope, q_rope = mla_queries(u[..., OFF_Q:OFF_KV], lp["q_norm_g"], lp["w_uq"], rope)
    if blocked:
        att = blocked_attend(q_nope, q_rope, *keys)
    else:
        att = attend(q_nope, q_rope, *keys).reshape(B, L, MLA_W)
    mla = att * jax.nn.silu(u[..., OFF_MLA_G:OFF_POOL])
    pool = pool_mix(u[..., OFF_POOL:OFF_POOL_G], lp["w_pool"], lp["pool_scale"]) * jax.nn.silu(u[..., OFF_POOL_G:])
    return jnp.concatenate([hy, mla, pool], axis=-1)

def setup_inputs(seed: int = 0) -> dict:
    key = jax.random.key(seed)
    ks = jax.random.split(key, 25)

    def nrm(k, shape, scale):
        return jax.random.normal(k, shape, jnp.float32) * scale

    return {
        "x": nrm(ks[0], (BATCH, SEQ, D_MODEL), 1.0),
        "c": nrm(ks[1], (BATCH, D_MODEL), 1.0),
        "ctx": nrm(ks[2], (BATCH, CTX_LEN, D_MODEL), 1.0),
        "c_ctx": nrm(ks[3], (D_MODEL,), 1.0),
        "norm_g": 1.0 + nrm(ks[4], (DEPTH, D_MODEL), 0.02),
        "w_ada": nrm(ks[5], (DEPTH, D_MODEL, 3 * D_MODEL), 0.5 * D_MODEL ** -0.5),
        "b_ada": nrm(ks[6], (DEPTH, 3 * D_MODEL), 0.02),
        "w_in": nrm(ks[7], (DEPTH, D_MODEL, N_IN), D_MODEL ** -0.5),
        "hy_conv_w": nrm(ks[8], (DEPTH, SHORT_CONV, 3 * HY_W), SHORT_CONV ** -0.5),
        "hy_conv_b": nrm(ks[9], (DEPTH, 3 * HY_W), 0.02),
        "hf_w1": nrm(ks[10], (DEPTH, FILTER_EMB, FILTER_HIDDEN), FILTER_EMB ** -0.5),
        "hf_b1": nrm(ks[11], (DEPTH, FILTER_HIDDEN), 0.02),
        "hf_freq": 1.0 + nrm(ks[12], (DEPTH, FILTER_HIDDEN), 0.02),
        "hf_w2": nrm(ks[13], (DEPTH, FILTER_HIDDEN, FILTER_HIDDEN), FILTER_HIDDEN ** -0.5),
        "hf_b2": nrm(ks[14], (DEPTH, FILTER_HIDDEN), 0.02),
        "hf_w3": nrm(ks[15], (DEPTH, FILTER_HIDDEN, 4 * HY_W), FILTER_HIDDEN ** -0.5),
        "hy_bias": nrm(ks[16], (DEPTH, 2, HY_W), 0.1),
        "q_norm_g": 1.0 + nrm(ks[17], (DEPTH, Q_RANK), 0.02),
        "w_uq": nrm(ks[18], (DEPTH, Q_RANK, MLA_HEADS * (MLA_DN + MLA_DR)), Q_RANK ** -0.5),
        "kv_norm_g": 1.0 + nrm(ks[19], (DEPTH, KV_RANK), 0.02),
        "w_ukv": nrm(ks[20], (DEPTH, KV_RANK, MLA_HEADS * (MLA_DN + MLA_DV)), KV_RANK ** -0.5),
        "w_pool": nrm(ks[21], (DEPTH, N_POOL_GROUPS, POOL_GROUP, POOL_GROUP), POOL_GROUP ** -0.5),
        "pool_scale": 1.0 + nrm(ks[22], (DEPTH, POOL_W), 0.1),
        "w_out": nrm(ks[23], (DEPTH, MIX_W, D_MODEL), MIX_W ** -0.5),
        "final_norm_g": 1.0 + nrm(ks[24], (D_MODEL,), 0.02),
    }

def reference(x, c, ctx, c_ctx, norm_g, w_ada, b_ada, w_in, hy_conv_w, hy_conv_b,
              hf_w1, hf_b1, hf_freq, hf_w2, hf_b2, hf_w3, hy_bias,
              q_norm_g, w_uq, kv_norm_g, w_ukv, w_pool, pool_scale, w_out, final_norm_g):
    rope = rope_tables(x.shape[1])
    x_l, x_c = x, ctx
    for l in range(DEPTH):
        last = l == DEPTH - 1
        lp = {"hy_conv_w": hy_conv_w[l], "hy_conv_b": hy_conv_b[l],
              "hf_w1": hf_w1[l], "hf_b1": hf_b1[l], "hf_freq": hf_freq[l],
              "hf_w2": hf_w2[l], "hf_b2": hf_b2[l], "hf_w3": hf_w3[l], "hy_bias": hy_bias[l],
              "q_norm_g": q_norm_g[l], "w_uq": w_uq[l],
              "w_pool": w_pool[l], "pool_scale": pool_scale[l]}
        sh, sc, gt = adaln(c, w_ada[l], b_ada[l])
        sh_c, sc_c, gt_c = adaln(c_ctx[None], w_ada[l], b_ada[l])
        h_l = rmsnorm(x_l, norm_g[l]) * (1.0 + sc) + sh
        h_c = rmsnorm(x_c, norm_g[l]) * (1.0 + sc_c) + sh_c
        u_l = h_l @ w_in[l]
        if last:
            u_c = h_c @ w_in[l][:, OFF_KV:OFF_MLA_G]
            u_c_kvr = u_c
        else:
            u_c = h_c @ w_in[l]
            u_c_kvr = u_c[..., OFF_KV:OFF_MLA_G]
        k_c = mla_keys(u_c_kvr, kv_norm_g[l], w_ukv[l], None)
        k_l = mla_keys(u_l[..., OFF_KV:OFF_MLA_G], kv_norm_g[l], w_ukv[l], rope)
        keys_all = (jnp.concatenate([k_l[0], k_c[0]], axis=1),
                    jnp.concatenate([k_l[1], k_c[1]], axis=1),
                    jnp.concatenate([k_l[2], k_c[2]], axis=1))
        out_l = mixer(u_l, keys_all, lp, rope, True)
        if not last:
            out_c = mixer(u_c, k_c, lp, None, False)
            x_c = x_c + gt_c * (out_c @ w_out[l])
        x_l = x_l + gt * (out_l @ w_out[l])
    return rmsnorm(x_l, final_norm_g)


_drawn_inputs = setup_inputs


def setup_inputs(seed=0):
    import zlib

    import numpy as np

    out = dict(_drawn_inputs(seed))
    spreads = {}
    factors = {'ctx': 8.0,
     'c_ctx': 4.641,
     'norm_g': 6.443,
     'hy_conv_b': 10.438,
     'hf_b1': 3.376,
     'hf_freq': 8.0,
     'hf_b2': 2.73,
     'q_norm_g': 52.717,
     'w_uq': 5.115,
     'kv_norm_g': 64.0,
     'pool_scale': 23.463,
     'final_norm_g': 8.164}
    for name, (base, spread) in spreads.items():
        noise = np.random.default_rng([zlib.crc32(name.encode()), seed]).standard_normal(out[name].shape)
        drawn = base * np.exp(spread * noise) if base else spread * noise
        out[name] = __import__('jax').numpy.asarray(drawn.astype(out[name].dtype))
    for name, factor in factors.items():
        out[name] = (out[name] * factor).astype(out[name].dtype)
    return out
```

```python
import math
from contextlib import ExitStack

import numpy as np

import concourse.bass as bass
from concourse import mybir

F32 = mybir.dt.float32
F32R = mybir.dt.float32r
ALU = mybir.AluOpType
ACT = mybir.ActivationFunctionType
AX = mybir.AxisListType

P = 128
D = 2048
KT = D // P
L = 512
LC = 256
LK = L + LC
EPS = 1e-6
HEADS, DN, DR, DV = 8, 128, 64, 128
SCALE = (DN + DR) ** -0.5
HF = L // 2

P_BSH, P_BSC, P_BG, P_NG = 0, 16, 32, 48
P_CW, P_CB, P_HB, P_QG, P_KG, P_PS = 64, 100, 112, 120, 124, 126
N_PAR = 130

T_V, T_X1, T_X2, T_POOL, T_Q = 1, 5, 9, 13, 17
U_KV = 21 * L
U_COLS = U_KV + 3 * LK

A_TILES = 5
B_GROUPS = 17
CH = 4
KW = 4


MAGIC = 1.5 * 2.0 ** 23
TWO_PI = (6.28125, 0.0019340515136719, 1.2556659e-06)
PI_MAX = 3.1415925


def project(nc, mem, t):
    par, U, UG, gcol = mem["par"], mem["U"], mem["UG"], mem["gcol"]
    with ExitStack() as ctx:
        def alloc(name, cols, dt=F32):
            return ctx.enter_context(nc.sbuf_tensor(name, [P, cols], dt))

        def sem(name):
            return ctx.enter_context(nc.semaphore(name))

        h_hi, h_lo = alloc("h_hi", KT * L, F32R), alloc("h_lo", KT * L, F32R)
        raw = alloc("w_raw", KW * CH * 256)
        w_hi, w_lo = alloc("w_hi", 2 * CH * 256, F32R), alloc("w_lo", 2 * CH * 256, F32R)
        wa_hi, wa_lo = alloc("wa_hi", 2 * A_TILES * P, F32R), alloc("wa_lo", 2 * A_TILES * P, F32R)
        c_hi, c_lo = alloc("hc_hi", 2 * LC, F32R), alloc("hc_lo", 2 * LC, F32R)
        tmp = alloc("h_tmp", 2 * LK)
        rstd = alloc("rstd", LK)
        cond, silu_c, parts = alloc("cond", 2 * KT), alloc("silu_c", 2 * KT), alloc("silu_parts", 4 * KT, F32R)
        mod, mod1 = alloc("mod", 2 * 4), alloc("mod1", 2 * 2)
        rows, comb = alloc("mod_rows", 256), alloc("comb", 2)
        ones, eps = mem["ones"], mem["eps"]
        ps = [ctx.enter_context(nc.psum_tensor(f"pp{i}", [P, 512], F32)) for i in range(8)]
        AW = A_TILES * P

        def x_tile(k):
            return UG[:, bass.ts(k, L)]

        def c_tile(k):
            return raw[:, bass.ts(k, LC)]

        def ada_ring(s):
            return U[:, 3 * L + s * 4096:3 * L + (s + 1) * 4096]

        def wa_raw(s):
            return U[:, s * AW:(s + 1) * AW]

        def lane(x, s, n=1024, pitch=1024):
            return x[:, s * pitch:s * pitch + n]

        gate_raw = tmp[:, 0:1024]
        gate_hi, gate_lo = wa_hi[:, 0:1024], wa_lo[:, 0:1024]

        x_in = [sem(f"x_in{i}") for i in range(4)]
        c_in = [sem(f"c_in{i}") for i in range(2)]
        par_in, cond_in, const = sem("par_in"), sem("cond_in"), sem("const")
        ada_in = [sem(f"ada_in{s}") for s in range(2)]
        wa_in = [sem(f"wa_in{s}") for s in range(2)]
        wb_in = [sem(f"wb_in{s}") for s in range(KW)]
        gate_in = sem("gate_in")
        silu_done, parts_done = sem("silu_done"), sem("silu_parts_done")
        sq_done, sum_done = sem("sq_done"), sem("sum_done")
        total_done, root_done, rstd_done = sem("total_done"), sem("root_done"), sem("rstd_done")
        ada_hi_done, ada_lo_done, ada_mm = sem("ada_hi_done"), sem("ada_lo_done"), sem("ada_mm")
        rows_done, comb_mm = sem("rows_done"), sem("comb_mm")
        mod_done, scaled = sem("mod_done"), sem("scaled")
        h_hi_done, h_lo_done = sem("h_hi_done"), sem("h_lo_done")
        wa_hi_done, wa_lo_done = sem("wa_hi_done"), sem("wa_lo_done")
        mmA_done, evA_done = sem("mmA_done"), sem("evA_done")
        wb_hi_done, wb_lo_done = sem("wb_hi_done"), sem("wb_lo_done")
        ev_done, mmc_done = sem("ev_done"), sem("mmc_done")
        gate_hi_done, gate_lo_done, gate_mm = sem("gate_hi_done"), sem("gate_lo_done"), sem("gate_mm")
        gate_rows, gate_comb, gate_done = sem("gate_rows_out"), sem("gate_comb"), sem("gate_done")
        dve_step = sem("dve_step_p")

        def bodies(eng, body):
            body(0, 0)
            with eng.Fori(0, 6) as i:
                body(2 * i + 1, 1)
                body(2 * i + 2, 0)
            body(13, 1)
            body(14, 0)
            body(15, 1)

        def has(j, ahead):
            return not isinstance(j, int) or j + ahead < KT

        block = ctx.enter_context(nc.Block())

        @block.sync
        def _(eng):
            eng.dma_start(cond[:], t["cond"]).then_inc(cond_in, 16)

            def load(j, s, early=False):
                if not early:
                    eng.wait_ge(ada_lo_done, 4 * j - 4)
                eng.dma_start(ada_ring(s), t["w_ada"][bass.ds(j, 1), :, :].rearrange("a p n -> p (a n)")).then_inc(ada_in[s], 16)
                if not early:
                    eng.wait_ge(wa_lo_done, j - 1)
                eng.dma_start(wa_raw(s), t["wa"][bass.ds(j, 1), :, :].rearrange("a p n -> p (a n)")).then_inc(wa_in[s], 16)

            load(0, 0, True)
            eng.dma_start(par[:], t["par"]).then_inc(par_in, 16)
            eng.dma_start(mem["ident"][:], t["ident"]).then_inc(par_in, 16)
            eng.dma_start(comb[0:4, :], t["comb"]).then_inc(par_in, 16)
            load(1, 1, True)
            with eng.Fori(1, KT // 2) as i:
                load(2 * i, 0)
                load(2 * i + 1, 1)

            def load_b(n, s, first=False):
                if first:
                    eng.wait_ge(h_lo_done, KT)
                else:
                    eng.wait_ge(wb_lo_done, n - KW + 1)
                eng.dma_start(raw[:, s * 1024:(s + 1) * 1024],
                              t["wb"][bass.ds(n, 1), :, :].rearrange("a p n -> p (a n)")).then_inc(wb_in[s], 16)

            def load_gate(m, first=False):
                if not first:
                    eng.wait_ge(gate_lo_done, m)
                eng.dma_start(gate_raw, t["w_gate"][bass.ds(m, 1), :, :].rearrange("a p n -> p (a n)")).then_inc(gate_in, 16)

            for s in range(KW):
                load_b(s, s, True)
            load_gate(0, True)
            with eng.Fori(1, 9) as i:
                for s in range(KW):
                    load_b(KW * i + s, s)
            for s in range(KW):
                load_b(36 + s, s)
                load_gate(s + 1)
            with eng.Fori(1, 7) as i:
                for s in range(KW):
                    load_b(36 + KW * i + s, s)
                    load_gate(KW * i + s + 1)
            for s in range(KW):
                load_b(64 + s, s)
                if s < 3:
                    load_gate(29 + s)

        @block.gpsimd
        def _(eng):
            def cut(j, s):
                eng.wait_ge(wa_hi_done, j + 1)
                eng.tensor_tensor(lane(wa_lo, s, AW, AW), wa_raw(s), lane(wa_hi, s, AW, AW), ALU.subtract).then_inc(wa_lo_done, 1)

            with eng.Fori(0, KT // 2) as i:
                cut(2 * i, 0)
                cut(2 * i + 1, 1)

        @block.scalar
        def _(eng):
            for i in range(4):
                eng.dma_start(UG[:, i * 2048:(i + 1) * 2048], t["xT"][:, i * 2048:(i + 1) * 2048]).then_inc(x_in[i], 16)
                if i % 2:
                    h = i // 2
                    eng.dma_start(raw[:, h * 2048:(h + 1) * 2048], t["cT"][:, h * 2048:(h + 1) * 2048]).then_inc(c_in[h], 16)

            def piece(j, i, s, early=False):
                n = 4 * j + i
                eng.wait_ge(ada_in[s], 8 * (j - s) + 16)
                if not early:
                    eng.wait_ge(ada_mm, n - 1)
                eng.activation(lane(w_hi, i % 2), ada_ring(s)[:, i * 1024:(i + 1) * 1024], ACT.Copy).then_inc(ada_hi_done, 1)

            def tokens(j, s, early=False):
                if not early:
                    eng.wait_ge(mmA_done, j - 1)
                eng.wait_ge(scaled, j + 1)
                eng.activation(h_hi[:, bass.ts(j, L)], tmp[:, s * LK:s * LK + L], ACT.Identity,
                               bias=mod[:, 4 * s:4 * s + 1], scale=1.0)
                eng.activation(lane(c_hi, s, LC, LC), tmp[:, s * LK + L:(s + 1) * LK], ACT.Identity,
                               bias=mod[:, 4 * s + 1:4 * s + 2], scale=1.0).then_inc(h_hi_done, 1)

            def rows_of_w(j, s):
                eng.wait_ge(wa_in[s], 8 * (j - s) + 16)
                eng.activation(lane(wa_hi, s, AW, AW), wa_raw(s), ACT.Copy).then_inc(wa_hi_done, 1)

            eng.wait_ge(cond_in, 16)
            eng.activation(silu_c[:], cond[:], ACT.Silu).then_inc(silu_done, 1)
            eng.wait_ge(silu_done, 1)
            eng.activation(parts[:].rearrange("p (k r) -> p k r", r=4)[:, :, 0:2],
                           silu_c[:].rearrange("p (k r) -> p k r", r=2), ACT.Copy).then_inc(parts_done, 1)
            for i in range(4):
                piece(0, i, 0, i < 2)
            for k in range(KT):
                eng.wait_ge(x_in[k // 4], 16)
                eng.wait_ge(c_in[k // 8], 16)
                if k >= 2:
                    eng.wait_ge(sum_done, k - 1)
                s = k % 2
                eng.activation(tmp[:, s * LK:s * LK + L], x_tile(k), ACT.Square)
                eng.activation(tmp[:, s * LK + L:(s + 1) * LK], c_tile(k), ACT.Square).then_inc(sq_done, 1)
            piece(1, 0, 1)
            piece(1, 1, 1)
            rows_of_w(0, 0)
            eng.wait_ge(total_done, 1)
            eng.wait_ge(const, 2)
            eng.wait_ge(sum_done, KT)
            eng.activation(tmp[:, 0:L], ps[5][:], ACT.Sqrt, bias=eps[:, 0:1], scale=1.0 / D)
            eng.activation(tmp[:, L:LK], ps[6][:, 0:LC], ACT.Sqrt, bias=eps[:, 0:1], scale=1.0 / D).then_inc(root_done, 1)
            piece(1, 2, 1)
            piece(1, 3, 1)
            piece(2, 0, 0)
            tokens(0, 0, True)

            def body(j, s):
                if has(j, 2):
                    piece(j + 2, 1, s)
                    piece(j + 2, 2, s)
                if has(j, 1):
                    tokens(j + 1, 1 - s, isinstance(j, int) and j == 0)
                if has(j, 2):
                    piece(j + 2, 3, s)
                if has(j, 1):
                    rows_of_w(j + 1, 1 - s)
                if has(j, 3):
                    piece(j + 3, 0, 1 - s)

            bodies(eng, body)

            eng.wait_ge(mmA_done, KT)
            eng.activation(U[:, L:2 * L], ps[0][:], ACT.Copy)
            eng.activation(U[:, 2 * L:3 * L], ps[1][:], ACT.Copy).then_inc(evA_done, 1)

            def context(i):
                eng.activation(U[:, U_KV + i * LK:U_KV + i * LK + L], ps[2 + i][:], ACT.Copy)
                eng.activation(U[:, U_KV + i * LK + L:U_KV + (i + 1) * LK],
                               ps[5 + i // 2][:, (i % 2) * LC:(i % 2 + 1) * LC], ACT.Copy).then_inc(evA_done, 1)

            def high_b(n, s, r, early=False):
                eng.wait_ge(wb_in[r], 4 * (n - r) + 16)
                if not early:
                    eng.wait_ge(mmc_done, n - 1)
                eng.activation(lane(w_hi, s), raw[:, r * 1024:(r + 1) * 1024], ACT.Copy).then_inc(wb_hi_done, 1)

            def high_gate(m, early=False):
                eng.wait_ge(gate_in, 16 * m + 16)
                if not early:
                    eng.wait_ge(gate_mm, m)
                eng.activation(gate_hi, gate_raw, ACT.Copy).then_inc(gate_hi_done, 1)

            def evacuate(g, pset, dst):
                eng.wait_ge(mmc_done, 4 * g + 4)
                for i in range(2):
                    ins = eng.activation(dst(i), ps[2 * pset + i][:], ACT.Copy)
                ins.then_inc(ev_done, 1)

            def to_u(g):
                return lambda i: U[:, bass.ts(3 + 2 * g + i, L)]

            def to_gate(g):
                return lambda i: UG[:, bass.ts(2 * (g - 9) + i, L)]

            def group(g, gp, prev, q=None, early=False):
                for c in range(CH):
                    high_b(4 * g + c, c % 2, c, early and c < 2)
                    if q is not None:
                        high_gate(4 * q + c, isinstance(q, int) and q == 0 and c == 0)
                    if c == 1 and prev is not None:
                        evacuate(g - 1, 1 - gp, prev)
                    if early and c < 3:
                        context(c)

            group(0, 0, None, early=True)
            with eng.Fori(0, 4) as i:
                group(2 * i + 1, 1, to_u(2 * i))
                group(2 * i + 2, 0, to_u(2 * i + 1))
            group(9, 1, to_u(8), 0)
            group(10, 0, to_gate(9), 1)
            with eng.Fori(1, 4) as i:
                group(2 * i + 9, 1, to_gate(2 * i + 8), 2 * i)
                group(2 * i + 10, 0, to_gate(2 * i + 9), 2 * i + 1)
            evacuate(16, 0, to_gate(16))

        @block.vector
        def _(eng):
            eng.memset(ones[:], 1.0).then_inc(const, 1)
            eng.memset(eps[:], EPS).then_inc(const, 1)

            def piece(j, i, s):
                eng.wait_ge(ada_hi_done, 4 * j + i + 1)
                eng.tensor_tensor(lane(w_lo, i % 2), ada_ring(s)[:, i * 1024:(i + 1) * 1024], lane(w_hi, i % 2),
                                  ALU.subtract).then_inc(ada_lo_done, 1)

            def rows_out(j):
                eng.wait_ge(ada_mm, 4 * j + 4)
                eng.tensor_copy(rows[0:4, :], ps[7][0:4, 0:256]).then_inc(rows_done, 1)

            def modulation(j, s):
                m, m1 = mod[:, 4 * s:4 * s + 4], mod1[:, 2 * s:2 * s + 2]
                eng.wait_ge(comb_mm, j + 1)
                eng.tensor_scalar(m1, ps[7][:, 258:260], par[:, bass.ds(P_BSC + j, 1)], 1.0, ALU.add, ALU.add).then_inc(dve_step, 1)
                eng.tensor_scalar(m[:, 0:2], ps[7][:, 256:258], par[:, bass.ds(P_BSH + j, 1)], None, ALU.add).then_inc(mod_done, 1)
                eng.wait_ge(dve_step, 2 * j + 1)
                eng.tensor_scalar(m[:, 2:4], m1, par[:, bass.ds(P_NG + j, 1)], None, ALU.mult).then_inc(dve_step, 1)

            def scale(j, s):
                m = mod[:, 4 * s:4 * s + 4]
                eng.wait_ge(dve_step, 2 * j + 2)
                eng.wait_ge(mod_done, j + 1)
                eng.scalar_tensor_tensor(out=tmp[:, s * LK:s * LK + L], in0=x_tile(j), scalar=m[:, 2:3],
                                         in1=rstd[:, 0:L], op0=ALU.mult, op1=ALU.mult)
                eng.scalar_tensor_tensor(out=tmp[:, s * LK + L:(s + 1) * LK], in0=c_tile(j), scalar=m[:, 3:4],
                                         in1=rstd[:, L:LK], op0=ALU.mult, op1=ALU.mult).then_inc(scaled, 1)

            def tokens(j, s):
                m = mod[:, 4 * s:4 * s + 4]
                eng.wait_ge(scaled, j + 1)
                eng.wait_ge(h_hi_done, j + 1)
                eng.scalar_tensor_tensor(out=h_lo[:, bass.ts(j, L)], in0=tmp[:, s * LK:s * LK + L], scalar=m[:, 0:1],
                                         in1=h_hi[:, bass.ts(j, L)], op0=ALU.add, op1=ALU.subtract)
                eng.scalar_tensor_tensor(out=lane(c_lo, s, LC, LC), in0=tmp[:, s * LK + L:(s + 1) * LK],
                                         scalar=m[:, 1:2], in1=lane(c_hi, s, LC, LC),
                                         op0=ALU.add, op1=ALU.subtract).then_inc(h_lo_done, 1)

            eng.wait_ge(parts_done, 1)
            pv = parts[:].rearrange("p (k r) -> p k r", r=4)
            eng.tensor_tensor(pv[:, :, 2:4], silu_c[:].rearrange("p (k r) -> p k r", r=2), pv[:, :, 0:2],
                              ALU.subtract).then_inc(parts_done, 1)
            for i in range(4):
                piece(0, i, 0)
            rows_out(0)
            eng.wait_ge(par_in, 48)
            for k in range(KT):
                eng.wait_ge(sq_done, k + 1)
                s = k % 2
                if k == 0:
                    eng.tensor_copy(rstd[:], tmp[:, 0:LK]).then_inc(sum_done, 1)
                else:
                    eng.wait_ge(sum_done, k)
                    eng.tensor_tensor(rstd[:], rstd[:], tmp[:, s * LK:(s + 1) * LK], ALU.add).then_inc(sum_done, 1)
            modulation(0, 0)
            piece(1, 0, 1)
            piece(1, 1, 1)
            eng.wait_ge(root_done, 1)
            eng.reciprocal(rstd[:], tmp[:, 0:LK]).then_inc(rstd_done, 1)
            eng.wait_ge(rstd_done, 1)
            scale(0, 0)
            piece(1, 2, 1)
            piece(1, 3, 1)
            rows_out(1)
            piece(2, 0, 0)
            tokens(0, 0)

            def body(j, s):
                if has(j, 1):
                    modulation(j + 1, 1 - s)
                if has(j, 2):
                    piece(j + 2, 1, s)
                if has(j, 1):
                    scale(j + 1, 1 - s)
                if has(j, 2):
                    piece(j + 2, 2, s)
                if has(j, 1):
                    tokens(j + 1, 1 - s)
                if has(j, 2):
                    piece(j + 2, 3, s)
                    rows_out(j + 2)
                if has(j, 3):
                    piece(j + 3, 0, 1 - s)

            bodies(eng, body)

            def low_b(n, s, r):
                eng.wait_ge(wb_hi_done, n + 1)
                eng.tensor_tensor(lane(w_lo, s), raw[:, r * 1024:(r + 1) * 1024], lane(w_hi, s), ALU.subtract).then_inc(wb_lo_done, 1)

            with eng.Fori(0, 9) as i:
                for s in range(4):
                    low_b(4 * i + s, s % 2, s)

            def columns(q):
                eng.wait_ge(gate_comb, q + 1)
                eng.tensor_tensor(gcol[:, bass.ds(2 * q, 2)], ps[7][:, 256:260:2], par[:, bass.ds(P_BG + 2 * q, 2)],
                                  ALU.add).then_inc(gate_done, 1)

            def gates(q, first=False):
                for c in range(4):
                    low_b(36 + 4 * q + c, c % 2, c)
                    if c == 0 and not first:
                        columns(q - 1)
                    eng.wait_ge(gate_hi_done, 4 * q + c + 1)
                    eng.tensor_tensor(gate_lo, gate_raw, gate_hi, ALU.subtract).then_inc(gate_lo_done, 1)
                eng.wait_ge(gate_mm, 4 * q + 4)
                eng.tensor_copy(rows[0:4, :], ps[7][0:4, 0:256]).then_inc(gate_rows, 1)

            gates(0, True)
            with eng.Fori(1, 8) as q:
                gates(q)
            columns(7)

        @block.tensor
        def _(eng):
            def piece(j, i, whole=None):
                if i == 0 and whole is None:
                    eng.wait_ge(mod_done, j)
                    eng.wait_ge(dve_step, 2 * j - 1)
                eng.wait_ge(ada_lo_done, 4 * j + i + 1)
                for k in range(4):
                    kk = 4 * i + k
                    for n, w in enumerate((w_hi, w_lo)):
                        mm = eng.matmul(ps[7][0:4, 0:256], parts[:, 4 * kk:4 * kk + 4], lane(w, i % 2)[:, k * 256:(k + 1) * 256],
                                        start=(kk == 0 and n == 0), stop=(kk == KT - 1 and n == 1))
                mm.then_inc(ada_mm, 1)

            def combine(done, n, signal):
                eng.wait_ge(done, n)
                eng.matmul(ps[7][:, 256:258], rows[0:4, 0:P], comb[0:4, :], start=True, stop=True)
                eng.matmul(ps[7][:, 258:260], rows[0:4, P:2 * P], comb[0:4, :], start=True, stop=True).then_inc(signal, 1)

            def tile(i, j, s, first, last):
                hh, hl = h_hi[:, bass.ts(j, L)], h_lo[:, bass.ts(j, L)]
                ch, cl = lane(c_hi, s, LC, LC), lane(c_lo, s, LC, LC)
                a, b = (lane(w, s, AW, AW)[:, i * P:(i + 1) * P] for w in (wa_hi, wa_lo))
                for n, (w, x) in enumerate(((a, hh), (a, hl), (b, hh))):
                    mm = eng.matmul(ps[i][:], w, x, start=first and n == 0, stop=last and n == 2)
                if i >= 2:
                    o = ps[5 + (i - 2) // 2][:, (i % 2) * LC:(i % 2 + 1) * LC]
                    for n, (w, x) in enumerate(((a, ch), (a, cl), (b, ch))):
                        mm = eng.matmul(o, w, x, start=first and n == 0 and i != 3, stop=last and n == 2, skip_group_check=True)
                return mm

            eng.wait_ge(parts_done, 2)
            for i in range(4):
                piece(0, i, True)
            eng.wait_ge(par_in, 48)
            combine(rows_done, 1, comb_mm)
            eng.wait_ge(const, 1)
            eng.wait_ge(sum_done, KT)
            eng.matmul(ps[5][:], ones[:], rstd[:, 0:L], start=True, stop=True)
            eng.matmul(ps[6][:, 0:LC], ones[:], rstd[:, L:LK], start=True, stop=True).then_inc(total_done, 1)
            for i in range(4):
                piece(1, i)
            combine(rows_done, 2, comb_mm)
            eng.wait_ge(root_done, 1)

            def body(j, s):
                first, last = isinstance(j, int) and j == 0, isinstance(j, int) and j == KT - 1
                eng.wait_ge(wa_lo_done, j + 1)
                eng.wait_ge(h_lo_done, j + 1)
                for i in range(A_TILES):
                    mm = tile(i, j, s, first, last)
                    if i < 4 and has(j, 2):
                        piece(j + 2, i)
                mm.then_inc(mmA_done, 1)
                if has(j, 2):
                    combine(rows_done, j + 3, comb_mm)

            bodies(eng, body)

            def group(g, pset, early=False, q=None):
                if q is not None and not (isinstance(q, int) and q == 0):
                    combine(gate_rows, q, gate_comb)
                for c in range(CH):
                    n = 4 * g + c
                    s = c % 2
                    if c == 0:
                        if early:
                            eng.wait_ge(evA_done, 1 if pset == 0 else 3)
                        else:
                            eng.wait_ge(ev_done, g - 1)
                    eng.wait_ge(wb_lo_done, n + 1)
                    for k in range(CH):
                        kk = c * CH + k
                        hh, hl = h_hi[:, kk * L:(kk + 1) * L], h_lo[:, kk * L:(kk + 1) * L]
                        for i in range(2):
                            o = s * 1024 + k * 256 + i * P
                            for m, (w, x) in enumerate(((w_hi, hh), (w_hi, hl), (w_lo, hh))):
                                mm = eng.matmul(ps[2 * pset + i][:], w[:, o:o + P], x,
                                                start=(kk == 0 and m == 0), stop=(kk == KT - 1 and m == 2))
                        if k == 1 and q is not None:
                            if c == 0 and not (isinstance(q, int) and q == 0):
                                eng.wait_ge(gate_done, q)
                            eng.wait_ge(gate_lo_done, 4 * q + c + 1)
                            for kg in range(4):
                                kp = 4 * c + kg
                                for m, w in enumerate((gate_hi, gate_lo)):
                                    gm = eng.matmul(ps[7][0:4, 0:256], parts[:, 4 * kp:4 * kp + 4], w[:, kg * 256:(kg + 1) * 256],
                                                    start=(kp == 0 and m == 0), stop=(kp == KT - 1 and m == 1))
                            gm.then_inc(gate_mm, 1)
                    mm.then_inc(mmc_done, 1)

            group(0, 0, True)
            group(1, 1, True)
            group(2, 0)
            with eng.Fori(1, 4) as i:
                group(2 * i + 1, 1)
                group(2 * i + 2, 0)
            group(9, 1, q=0)
            with eng.Fori(1, 4) as i:
                group(2 * i + 8, 0, q=2 * i - 1)
                group(2 * i + 9, 1, q=2 * i)
            group(16, 0, q=7)
            combine(gate_rows, 8, gate_comb)


def hyena(nc, mem, t):
    par, U, UG = mem["par"], mem["U"], mem["UG"]
    ident, ones = mem["ident"], mem["ones"]
    with ExitStack() as ctx:
        def alloc(name, cols, dt=F32):
            return ctx.enter_context(nc.sbuf_tensor(name, [P, cols], dt))

        def sem(name):
            return ctx.enter_context(nc.semaphore(name))

        fwd_hi, fwd_lo = alloc("fwd_hi", 2048, F32R), alloc("fwd_lo", 2048, F32R)
        inv_hi, inv_lo = alloc("inv_hi", 2048, F32R), alloc("inv_lo", 2048, F32R)
        K = alloc("spectrum", 8 * L)
        g_hi, g_lo = alloc("g_hi", 8 * L, F32R), alloc("g_lo", 8 * L, F32R)
        Z = alloc("z_spec", 8 * L)
        zt_hi, zt_lo = alloc("zt_hi", 4 * L, F32R), alloc("zt_lo", 4 * L, F32R)
        T = alloc("temps", 4 * L)
        h2 = alloc("filter_hidden", L)
        hf = alloc("hf_params", 131)
        nrm, small = alloc("nrm", 8), alloc("hy_small", 8)
        ps = [ctx.enter_context(nc.psum_tensor(f"ph{i}", [P, 512], F32)) for i in range(8)]

        def tmp(i):
            return T[:, i * L:(i + 1) * L] if i < 4 else U[:, 12 * L:13 * L]

        def bias_of(c):
            return tmp(4 if c % 2 else 2)

        def taps_of(n):
            return K[:, 4 * (n % 2) * L:(4 * (n % 2) + 2) * L]

        def squares_of(n):
            return K[:, (4 * (n % 2) + 2) * L:(4 * (n % 2) + 4) * L]

        def tap_pair(x, l):
            return x[:, :].rearrange("p (d l c) -> p d l c", d=2, l=4)[:, :, l, :]

        def u(i):
            return U[:, i * L:(i + 1) * L]

        def halves(x, tile, half):
            return x[:, tile * L:(tile + 2) * L].rearrange("p (f c) -> p f c", f=2)[:, :, half * 256:(half + 1) * 256]

        def as2(x):
            return x.rearrange("p (f c) -> p f c", f=2)

        tab_in, dec_in, hf_in, feat_in = sem("tab_in"), sem("dec_in"), sem("hf_in"), sem("feat_in")
        tab_hi, tab_lo = sem("tab_hi"), sem("tab_lo")
        mlp_mm, mlp_arg, mlp_sin = sem("mlp_mm"), sem("mlp_arg"), sem("mlp_sin")
        silu_done, centre, conv_done = sem("gate_silu"), sem("centre_tap"), sem("conv_done")
        taps_mm, taps_sum, taps_hi, taps_sq, taps_lo = sem("taps_mm"), sem("taps_sum"), sem("taps_hi"), sem("taps_sq"), sem("taps_lo")
        norm_mm, norm_root, norm_done = sem("norm_mm"), sem("norm_root"), sem("norm_done")
        k_mm, k_odd, k_done = sem("k_mm"), sem("k_odd"), sem("k_done")
        tr_done, zt_hi_done, zt_lo_done = sem("tr_done"), sem("zt_hi_done"), sem("zt_lo_done")
        f_mm, f_odd, f_done = sem("f_mm"), sem("f_odd"), sem("f_done")
        g_sum, g_hi_done, g_lo_done = sem("g_sum"), sem("g_hi_done"), sem("g_lo_done")
        i_mm, bias_done, y_done = sem("i_mm"), sem("bias_done"), sem("y_done")
        sq_sum, mirror_done, g_lo_pool = sem("sq_sum"), sem("mirror_done"), sem("g_lo_pool")
        step, pool_step = sem("dve_step_h"), sem("pool_step_h")

        block = ctx.enter_context(nc.Block())

        @block.sync
        def _(eng):
            eng.dma_start(hf[0:64, :], t["hf"]).then_inc(hf_in, 16)
            eng.dma_start(T[0:33, 0:L], t["feats"]).then_inc(feat_in, 16)
            eng.dma_start(K[:, 0:4096], t["tables"]).then_inc(tab_in, 16)
            for o in range(2):
                if o:
                    eng.wait_ge(g_lo_done, 4)
                    eng.wait_ge(g_lo_pool, 4)
                eng.dma_start(Z[:, 0:5 * L], t["decay"]).then_inc(dec_in, 16)
                eng.dma_start(Z[0:64, 5 * L:7 * L], t["w3"][o, :, :]).then_inc(dec_in, 16)

        @block.gpsimd
        def _(eng):
            steps = [0]

            def link(ins):
                steps[0] += 1
                ins.then_inc(pool_step, 1)
                eng.wait_ge(pool_step, steps[0])

            def conv(i):
                if i == 4:
                    eng.wait_ge(conv_done, 4)
                eng.tensor_scalar(u(i), u(i + 1), par[:, P_CW + 12 + i:P_CW + 13 + i], par[:, P_CB + i:P_CB + i + 1],
                                  ALU.mult, ALU.add)
                before, after = par[:, P_CW + i:P_CW + i + 1], par[:, P_CW + 24 + i:P_CW + 25 + i]
                tb = tmp(2)[:, 0:L - 1]
                ta = tmp(3)[:, 0:L - 1]
                eng.tensor_scalar(ta, u(i + 1)[:, 0:L - 1], before, None, ALU.mult)
                link(eng.tensor_scalar(tb, u(i + 1)[:, 1:L], after, None, ALU.mult))
                link(eng.tensor_tensor(u(i)[:, 1:L], u(i)[:, 1:L], ta, ALU.add))
                link(eng.tensor_tensor(u(i)[:, 0:L - 1], u(i)[:, 0:L - 1], tb, ALU.add))

            eng.wait_ge(tab_hi, 1)
            eng.tensor_tensor(fwd_lo[:], K[:, 0:2048], fwd_hi[:], ALU.subtract).then_inc(tab_lo, 1)
            eng.wait_ge(tab_hi, 2)
            eng.tensor_tensor(inv_lo[:], K[:, 2048:4096], inv_hi[:], ALU.subtract).then_inc(tab_lo, 1)
            for i in range(4, 10):
                conv(i)
            for o in range(2):
                for l in range(4 * o):
                    eng.wait_ge(taps_sq, 4 * o + l + 1)
                    sq = squares_of(l)
                    eng.tensor_tensor(sq[:, 0:L], sq[:, 0:L], sq[:, L:2 * L], ALU.add).then_inc(sq_sum, 1)
                for hf_ in range(2):
                    n = 2 * o + hf_
                    zz = [Z[:, (4 * hf_ + i) * L:(4 * hf_ + i + 1) * L] for i in range(4)]
                    eng.wait_ge(f_done, 2 * n + 2)
                    c, s = as2(zz[2]), as2(zz[3])
                    kc, ks = halves(K, 4, hf_), halves(K, 6, hf_)
                    ta, tb = as2(tmp(3)), as2(tmp(4))
                    eng.tensor_tensor(ta, c, ks, ALU.mult)
                    link(eng.tensor_tensor(tb, s, ks, ALU.mult))
                    eng.tensor_tensor(c, c, kc, ALU.mult)
                    link(eng.tensor_tensor(s, s, kc, ALU.mult))
                    eng.tensor_tensor(c, c, tb, ALU.subtract)
                    eng.tensor_tensor(s, s, ta, ALU.add).then_inc(mirror_done, 1)
                    eng.wait_ge(mirror_done, n + 1)
                    for g in (2, 3):
                        eng.wait_ge(g_sum, 4 * n + g + 1)
                        eng.wait_ge(g_hi_done, 4 * n + g + 1)
                        src = (tmp(1), zz[3])[g - 2]
                        eng.tensor_tensor(halves(g_lo, 2 * g, hf_), as2(src), halves(g_hi, 2 * g, hf_), ALU.subtract).then_inc(g_lo_pool, 1)

        @block.scalar
        def _(eng):
            def turned(o, half):
                for b in range(2):
                    eng.wait_ge(tr_done, 2 * (2 * o + half) + b + 1)
                    dst = zt_hi[:, 2 * b * L:(2 * b + 2) * L].rearrange("p (t c) -> p t c", t=2)[:, :, half * 256:(half + 1) * 256]
                    eng.activation(dst, as2(ps[4 + 2 * half + b][:]), ACT.Copy).then_inc(zt_hi_done, 1)

            def centre_tap(i):
                eng.activation(u(i), u(i + 1), ACT.Identity, bias=par[:, P_CB + i:P_CB + i + 1],
                               scale=par[:, P_CW + 12 + i:P_CW + 13 + i]).then_inc(centre, 1)

            for i in range(4):
                if i >= 1:
                    eng.wait_ge(conv_done, i)
                centre_tap(i)
            eng.wait_ge(tab_in, 16)
            eng.activation(fwd_hi[:], K[:, 0:2048], ACT.Copy).then_inc(tab_hi, 1)
            turned(0, 0)
            turned(0, 1)
            eng.wait_ge(mlp_arg, 1)
            eng.activation(T[0:64, 0:L], T[0:64, L:2 * L], ACT.Sin).then_inc(mlp_sin, 1)
            eng.activation(inv_hi[:], K[:, 2048:4096], ACT.Copy).then_inc(tab_hi, 1)
            eng.wait_ge(mlp_arg, 2)
            eng.activation(h2[0:64, 0:L], T[0:64, L:2 * L], ACT.Sin).then_inc(mlp_sin, 1)
            for o in range(2):
                if o:
                    turned(o, 0)
                    turned(o, 1)
                for l in range(4):
                    n = 4 * o + l
                    eng.wait_ge(taps_sum, n + 1)
                    eng.activation(tap_pair(g_hi, l), as2(taps_of(n)), ACT.Copy).then_inc(taps_hi, 1)
                    if l >= 2:
                        eng.wait_ge(norm_mm, n - 1)
                    eng.activation(squares_of(n), taps_of(n), ACT.Square).then_inc(taps_sq, 1)
                eng.wait_ge(norm_mm, 4 * o + 4)
                eng.activation(small[:, 0:4], ps[6][:, 0:4], ACT.Sqrt, bias=mem["eps"][:, 0:1], scale=0.5).then_inc(norm_root, 1)
                part = UG[:, 4096 * o:4096 * (o + 1)]
                eng.activation(part, part, ACT.Silu).then_inc(silu_done, 1)
                for m in range(4):
                    eng.wait_ge(k_mm, 4 * o + m + 1)
                    if m >= 2:
                        eng.wait_ge(k_done, 4 * o + m - 1)
                    eng.activation(tmp(m % 2), ps[2 * m + 1][:], ACT.Copy).then_inc(k_odd, 1)
                if o == 0:
                    eng.wait_ge(pool_step, 6 * 3)
                    centre_tap(10)
                    eng.wait_ge(conv_done, 5)
                    centre_tap(11)
                for hf_ in range(2):
                    n = 2 * o + hf_
                    for x in range(2):
                        eng.wait_ge(f_mm, 2 * n + x + 1)
                        if x == 0:
                            eng.wait_ge(k_done, 4 * o + 4)
                        if n == 0:
                            eng.wait_ge(pool_step, 6 * 3)
                        elif x == 0:
                            eng.wait_ge(f_done, 2 * n)
                        if x == 1 and n:
                            eng.wait_ge(g_lo_done, 2 * n)
                        eng.activation(tmp(0) if x else tmp(2), ps[4 * hf_ + 2 * x + 1][:], ACT.Copy).then_inc(f_odd, 1)
                    for g in range(4):
                        eng.wait_ge(g_sum, 4 * n + g + 1)
                        src = (tmp(0), Z[:, (4 * hf_ + 2) * L:(4 * hf_ + 3) * L], tmp(1), Z[:, (4 * hf_ + 3) * L:(4 * hf_ + 4) * L])[g]
                        eng.activation(halves(g_hi, 2 * g, hf_), as2(src), ACT.Copy).then_inc(g_hi_done, 1)
                for c in range(4):
                    n = 4 * o + c
                    if c >= 2:
                        eng.wait_ge(y_done, n - 1)
                    eng.activation(bias_of(c), u(c), ACT.Copy, scale=par[:, P_HB + 4 * o + c:P_HB + 4 * o + c + 1]).then_inc(bias_done, 1)

        @block.vector
        def _(eng):
            steps = [0]

            def link(ins):
                steps[0] += 1
                ins.then_inc(step, 1)
                eng.wait_ge(step, steps[0])

            def turned(o, half):
                for b in range(2):
                    eng.wait_ge(zt_hi_done, 2 * (2 * o + half) + b + 1)
                    hi, lo = (z[:, 2 * b * L:(2 * b + 2) * L].rearrange("p (t c) -> p t c", t=2)[:, :, half * 256:(half + 1) * 256]
                              for z in (zt_hi, zt_lo))
                    eng.tensor_tensor(lo, as2(ps[4 + 2 * half + b][:]), hi, ALU.subtract).then_inc(zt_lo_done, 1)

            def neighbour_taps(i, n):
                eng.wait_ge(centre, n)
                link(eng.scalar_tensor_tensor(out=u(i)[:, 1:L], in0=u(i + 1)[:, 0:L - 1], scalar=par[:, P_CW + i:P_CW + i + 1],
                                              in1=u(i)[:, 1:L], op0=ALU.mult, op1=ALU.add))
                eng.scalar_tensor_tensor(out=u(i)[:, 0:L - 1], in0=u(i + 1)[:, 1:L], scalar=par[:, P_CW + 24 + i:P_CW + 25 + i],
                                         in1=u(i)[:, 0:L - 1], op0=ALU.mult, op1=ALU.add).then_inc(conv_done, 1)

            for i in range(4):
                neighbour_taps(i, i + 1)
            eng.wait_ge(hf_in, 16)
            a, r = (T[0:64, i * L:(i + 1) * L] for i in (1, 0))
            for layer in range(2):
                eng.wait_ge(mlp_mm, layer + 1)
                bias = hf[0:64, 128:129] if layer == 0 else hf[0:64, 130:131]
                link(eng.tensor_scalar(a, ps[3][0:64, :], bias, hf[0:64, 129:130], ALU.add, ALU.mult))
                link(eng.tensor_scalar(r, a, 1.0 / (2 * math.pi), MAGIC, ALU.mult, ALU.add))
                link(eng.tensor_scalar(r, r, MAGIC, None, ALU.subtract))
                for part in TWO_PI:
                    link(eng.scalar_tensor_tensor(out=a, in0=r, scalar=-part, in1=a, op0=ALU.mult, op1=ALU.add))
                eng.tensor_scalar(a, a, -PI_MAX, PI_MAX, ALU.max, ALU.min).then_inc(mlp_arg, 1)
                if layer == 0:
                    turned(0, 0)
                    turned(0, 1)
            for o in range(2):
                if o:
                    turned(o, 0)
                    turned(o, 1)
                for l in range(4):
                    n = 4 * o + l
                    eng.wait_ge(taps_mm, n + 1)
                    if l == 0:
                        eng.wait_ge(dec_in, 32 * o + 32)
                        eng.wait_ge(mlp_sin, 2)
                        eng.wait_ge(tab_lo, 2)
                    eng.tensor_tensor(tmp(0), ps[2 * (l % 2)][:], Z[:, l * L:(l + 1) * L], ALU.mult)
                    dec = 4 if l == 0 else l
                    link(eng.tensor_tensor(tmp(1), ps[2 * (l % 2) + 1][:], Z[:, dec * L:(dec + 1) * L], ALU.mult))
                    if l >= 2:
                        eng.wait_ge(taps_sq, n - 1)
                        eng.wait_ge(taps_lo, n - 1)
                    both = taps_of(n)
                    eng.tensor_tensor(both[:, 0:L], tmp(0), tmp(1), ALU.add)
                    eng.tensor_tensor(both[:, L:2 * L], tmp(0), tmp(1), ALU.subtract).then_inc(taps_sum, 1)
                    eng.wait_ge(taps_sum, n + 1)
                    eng.wait_ge(taps_hi, n + 1)
                    eng.tensor_tensor(tap_pair(g_lo, l), as2(both), tap_pair(g_hi, l), ALU.subtract).then_inc(taps_lo, 1)
                eng.wait_ge(taps_lo, 4 * o + 4)
                eng.wait_ge(norm_root, o + 1)
                link(eng.reciprocal(small[:, 4:8], small[:, 0:4]))
                eng.tensor_scalar(nrm[:, 4 * o:4 * o + 4], small[:, 4:8], 1.0 / 512, None, ALU.mult).then_inc(norm_done, 1)
                for m in range(4):
                    ft, x = m // 2, m % 2
                    eng.wait_ge(k_odd, 4 * o + m + 1)
                    eng.tensor_tensor(K[:, (2 * x + ft) * L:(2 * x + ft + 1) * L], ps[2 * m][:], tmp(m % 2), ALU.add)
                    eng.tensor_tensor(K[:, (4 + 2 * x + ft) * L:(5 + 2 * x + ft) * L], ps[2 * m][:], tmp(m % 2), ALU.subtract).then_inc(k_done, 1)
                if o == 0:
                    neighbour_taps(10, 5)
                    neighbour_taps(11, 6)
                    eng.wait_ge(conv_done, 6)
                eng.wait_ge(k_done, 4 * o + 4)
                for hf_ in range(2):
                    n = 2 * o + hf_
                    zz = [Z[:, (4 * hf_ + i) * L:(4 * hf_ + i + 1) * L] for i in range(4)]
                    for x in range(2):
                        eng.wait_ge(f_odd, 2 * n + x + 1)
                        odd = tmp(0) if x else tmp(2)
                        eng.tensor_tensor(zz[x], ps[4 * hf_ + 2 * x][:], odd, ALU.add)
                        eng.tensor_tensor(zz[2 + x], ps[4 * hf_ + 2 * x][:], odd, ALU.subtract).then_inc(f_done, 1)
                    eng.wait_ge(f_done, 2 * n + 2)
                    if n:
                        eng.wait_ge(g_hi_done, 4 * n)
                        eng.wait_ge(g_lo_pool, 2 * n)
                    c, s = as2(zz[0]), as2(zz[1])
                    kc, ks = halves(K, 0, hf_), halves(K, 2, hf_)
                    ta, tb = as2(tmp(0)), as2(tmp(1))
                    eng.tensor_tensor(ta, c, ks, ALU.mult)
                    link(eng.tensor_tensor(tb, s, ks, ALU.mult))
                    eng.tensor_tensor(c, c, kc, ALU.mult)
                    link(eng.tensor_tensor(s, s, kc, ALU.mult))
                    eng.tensor_tensor(c, c, tb, ALU.subtract)
                    link(eng.tensor_tensor(s, s, ta, ALU.add))
                    eng.wait_ge(mirror_done, n + 1)
                    for x in range(2):
                        eng.tensor_tensor(tmp(x), zz[x], zz[2 + x], ALU.add).then_inc(g_sum, 1)
                        eng.tensor_tensor(zz[2 + x], zz[x], zz[2 + x], ALU.subtract).then_inc(g_sum, 1)
                    for g in range(2):
                        eng.wait_ge(g_sum, 4 * n + g + 1)
                        eng.wait_ge(g_hi_done, 4 * n + g + 1)
                        src = (tmp(0), zz[2])[g]
                        eng.tensor_tensor(halves(g_lo, 2 * g, hf_), as2(src), halves(g_hi, 2 * g, hf_), ALU.subtract).then_inc(g_lo_done, 1)
                eng.wait_ge(norm_done, o + 1)
                eng.wait_ge(g_lo_done, 4 * o + 4)
                if o == 0:
                    eng.wait_ge(pool_step, 6 * 3)
                for c in range(4):
                    n = 4 * o + c
                    eng.wait_ge(i_mm, n + 1)
                    eng.wait_ge(bias_done, n + 1)
                    y = ps[c][:].rearrange("p (r t) -> p t r", r=2)
                    link(eng.scalar_tensor_tensor(out=tmp(0).rearrange("p (t r) -> p t r", r=2), in0=y, scalar=nrm[:, n:n + 1],
                                                  in1=bias_of(c).rearrange("p (t r) -> p t r", r=2), op0=ALU.mult, op1=ALU.add))
                    if o == 0:
                        eng.tensor_tensor(u(c), tmp(0), u(4 + c), ALU.mult).then_inc(y_done, 1)
                        eng.wait_ge(y_done, n + 1)
                    else:
                        link(eng.tensor_tensor(tmp(0), tmp(0), u(8 + c), ALU.mult))
                        eng.wait_ge(silu_done, 2)
                        eng.tensor_tensor(UG[:, c * L:(c + 1) * L], tmp(0), UG[:, c * L:(c + 1) * L], ALU.mult).then_inc(y_done, 1)
                        eng.wait_ge(y_done, n + 1)

        @block.tensor
        def _(eng):
            eng.wait_ge(hf_in, 16)
            eng.wait_ge(feat_in, 16)
            eng.matmul(ps[3][0:64, :], hf[0:33, 0:64], T[0:33, 0:L], start=True, stop=True).then_inc(mlp_mm, 1)

            def transposes(o, half):
                if half == 0:
                    if o:
                        eng.wait_ge(y_done, 4)
                        eng.wait_ge(f_done, 4)
                    else:
                        eng.wait_ge(conv_done, 4)
                for b in range(2):
                    for jt in range(2):
                        for cc in range(2):
                            src = u(2 * half + cc)[:, b + 256 * jt:256 * (jt + 1):2]
                            mm = eng.transpose(ps[4 + 2 * half + b][:, jt * 256 + cc * P:jt * 256 + (cc + 1) * P], src, ident[:])
                    mm.then_inc(tr_done, 1)

            transposes(0, 0)
            transposes(0, 1)
            eng.wait_ge(mlp_sin, 1)
            eng.matmul(ps[3][0:64, :], hf[0:64, 64:128], T[0:64, 0:L], start=True, stop=True).then_inc(mlp_mm, 1)
            eng.wait_ge(mlp_sin, 2)

            def passes(dst, ws, xs, first, last):
                for m, (w, x) in enumerate(((ws[0], xs[0]), (ws[0], xs[1]), (ws[1], xs[0]))):
                    mm = eng.matmul(dst, w, x, start=first and m == 0, stop=last and m == 2)
                return mm

            for o in range(2):
                if o:
                    transposes(o, 0)
                    transposes(o, 1)
                eng.wait_ge(dec_in, 32 * o + 32)

                def taps(l):
                    n = 4 * o + l
                    if n >= 2:
                        eng.wait_ge(taps_sum, n - 1)
                    for d in range(2):
                        mm = eng.matmul(ps[2 * (l % 2) + d][:], h2[0:64, l * P:(l + 1) * P], Z[0:64, (5 + d) * L:(6 + d) * L],
                                        start=True, stop=True)
                    mm.then_inc(taps_mm, 1)

                taps(0)
                for l in range(4):
                    if l < 3:
                        taps(l + 1)
                    if l == 0:
                        eng.wait_ge(zt_lo_done, 4 * o + 4)
                    parts = [squares_of(l)[:, 0:L]]
                    if o:
                        eng.wait_ge(sq_sum, l + 1)
                    else:
                        eng.wait_ge(taps_sq, l + 1)
                        parts.append(squares_of(l)[:, L:2 * L])
                    for c in range(4):
                        for i, sq in enumerate(parts):
                            mm = eng.matmul(ps[6][:, c:c + 1], sq[:, c * P:(c + 1) * P], ones[:, 0:1],
                                            start=(l == 0 and c == 0 and i == 0), stop=(l == 3 and i == len(parts) - 1),
                                            skip_group_check=True)
                    mm.then_inc(norm_mm, 1)
                eng.wait_ge(taps_lo, 4 * o + 4)
                eng.wait_ge(taps_sum, 4 * o + 4)
                eng.wait_ge(norm_root, o + 1)
                eng.wait_ge(tab_lo, 2)
                for m in range(4):
                    ft, x = m // 2, m % 2
                    for pr in range(2):
                        for jt in range(2):
                            a = (2 * (2 * x + pr) + jt) * 256 + ft * P
                            b = (4 * x + 2 * pr + jt) * L
                            mm = passes(ps[2 * m + pr][:], (fwd_hi[:, a:a + P], fwd_lo[:, a:a + P]),
                                        (g_hi[:, b:b + L], g_lo[:, b:b + L]), jt == 0, jt == 1)
                    mm.then_inc(k_mm, 1)

                def forward(half):
                    eng.wait_ge(k_done, 4 * o + 2 * half + 2)
                    for x in range(2):
                        for pr in range(2):
                            for ft in range(2):
                                for jt in range(2):
                                    a = (2 * (2 * x + pr) + jt) * 256 + ft * P
                                    b = (2 * pr + jt) * L + half * 256
                                    mm = passes(ps[4 * half + 2 * x + pr][:, ft * 256:(ft + 1) * 256],
                                                (fwd_hi[:, a:a + P], fwd_lo[:, a:a + P]),
                                                (zt_hi[:, b:b + 256], zt_lo[:, b:b + 256]), jt == 0, jt == 1)
                        mm.then_inc(f_mm, 1)

                forward(0)
                forward(1)
                for c in range(4):
                    n = 4 * o + c
                    eng.wait_ge(g_lo_done, 4 * o + (2 if c < 2 else 4))
                    eng.wait_ge(g_lo_pool, 4 * o + (2 if c < 2 else 4))
                    for pr in range(2):
                        for i in range(4):
                            x, ft = i // 2, i % 2
                            a = (2 * (2 * x + pr) + ft) * L + c * P
                            b = (2 * (2 * x + pr) + ft) * 256
                            mm = passes(ps[c][:, pr * 256:(pr + 1) * 256], (g_hi[:, a:a + P], g_lo[:, a:a + P]),
                                        (inv_hi[:, b:b + 256], inv_lo[:, b:b + 256]), i == 0, i == 3)
                    mm.then_inc(i_mm, 1)


def attend(nc, mem, t):
    par, U, UG, ident, ones, eps = (mem[n] for n in ("par", "U", "UG", "ident", "ones", "eps"))
    with ExitStack() as ctx:
        def alloc(name, cols, dt=F32):
            return ctx.enter_context(nc.sbuf_tensor(name, [P, cols], dt))

        def sem(name):
            return ctx.enter_context(nc.semaphore(name))

        qn_hi, qn_lo = alloc("qn_hi", 4 * L, F32R), alloc("qn_lo", 4 * L, F32R)
        kv_hi, kv_lo = alloc("kv_hi", 2 * LK, F32R), alloc("kv_lo", 2 * LK, F32R)
        kr_hi, kr_lo = alloc("kr_hi", LK, F32R), alloc("kr_lo", LK, F32R)
        w_hi, w_lo = alloc("wh_hi", 2560, F32R), alloc("wh_lo", 2560, F32R)
        q_hi, q_lo = alloc("q_hi", 3 * L, F32R), alloc("q_lo", 3 * L, F32R)
        k_hi, k_lo = alloc("k_hi", 2 * LK, F32R), alloc("k_lo", 2 * LK, F32R)
        v_hi, v_lo = alloc("v_hi", 6 * 256, F32R), alloc("v_lo", 6 * 256, F32R)
        pt_hi, pt_lo = alloc("pt_hi", 6 * L, F32R), alloc("pt_lo", 6 * L, F32R)
        swap, wp, edge = alloc("swap", P), alloc("w_pool", 4 * P), alloc("edge", 64)
        st = alloc("softmax_stats", 8)
        psum = ctx.enter_context(nc.psum_tensor("pa", [P, 8, 512], F32))
        ps = [psum[:, i, :] for i in range(8)]

        def prob(s):
            return U[:, s * LK:(s + 1) * LK]

        rope_c, rope_s = U[:, 3 * L:4 * L], U[:, 4 * L:5 * L]
        ta, tb = U[:, 5 * L:6 * L], U[:, 6 * L:7 * L]
        r_kv = U[:, 7 * L:7 * L + LK]
        pads = [U[:, 9 * L + i * 528:9 * L + (i + 1) * 528] for i in range(3)]
        raw = U[:, T_Q * L:T_Q * L + 2560]

        def q_t(i):
            return U[:, (T_Q + i) * L:(T_Q + i + 1) * L]

        def kv_t(i):
            return U[:, U_KV + i * LK:U_KV + (i + 1) * LK]

        k_rope = U[:, U_KV + 2 * LK:U_KV + 3 * LK]

        tab_in, w_in = sem("rope_in"), sem("head_w_in")
        sq_done, sum_mm, root_done, rst_done = sem("sq_done_a"), sem("sum_mm"), sem("root_done_a"), sem("rst_done")
        kr_mm, kr_done, kr_cut = sem("kr_mm"), sem("kr_done"), sem("kr_cut")
        nrm_done, nrm_hi, nrm_lo = sem("nrm_done_a"), sem("nrm_hi"), sem("nrm_lo")
        wh_hi, wh_lo = sem("wh_hi_done"), sem("wh_lo_done")
        pr_mm, pr_hi, pr_lo = sem("pr_mm"), sem("pr_hi"), sem("pr_lo")
        qr_copy, qr_mm, qr_rot = sem("qr_copy"), sem("qr_mm"), sem("qr_rot")
        s_mm, max_done, e_done, p_done = sem("s_mm"), sem("max_done"), sem("e_done"), sem("p_done")
        t_mm, pt_hi_done, pt_lo_done, pv_mm, o_done = sem("t_mm"), sem("pt_hi_done"), sem("pt_lo_done"), sem("pv_mm"), sem("o_done")
        pool_step, pool_done, pool_mm, pool_out = sem("pool_step"), sem("pool_done"), sem("pool_mm"), sem("pool_out")
        step, st_max, st_rec = sem("dve_step_a"), sem("st_max"), sem("st_rec")

        block = ctx.enter_context(nc.Block())
        SQ = [(q_t(i), L) for i in range(4)] + [(kv_t(i), LK) for i in range(2)]

        @block.sync
        def _(eng):
            for dst, n in ((rope_c, "rope_c"), (rope_s, "rope_s"), (swap[:], "swap"), (wp[:], "w_pool"), (edge[:], "edge")):
                eng.dma_start(dst, t[n]).then_inc(tab_in, 16)

            def load(p, early=False):
                if early:
                    eng.wait_ge(nrm_lo, 6)
                else:
                    eng.wait_ge(wh_lo, 2 * p)
                eng.dma_start(raw, t["w_heads"][bass.ds(p, 1), :, :].rearrange("a p n -> p (a n)")).then_inc(w_in, 16)

            load(0, True)
            with eng.Fori(1, 4) as p:
                load(p)

        @block.gpsimd
        def _(eng):
            count = [0]

            def link(ins):
                count[0] += 1
                ins.then_inc(pool_step, 1)
                eng.wait_ge(pool_step, count[0])

            eng.wait_ge(tab_in, 80)
            for g in range(4):
                half = 1 << g
                x = U[:, (T_POOL + g) * L:(T_POOL + g + 1) * L]
                if g == 0:
                    link(eng.memset(pads[0], 0.0))
                link(eng.tensor_copy(pads[0][:, 8:8 + L], x))
                a, n = pads[0], 528
                for d in range(g + 1):
                    b = pads[1 + d % 2]
                    n -= 1 << d
                    link(eng.tensor_tensor(b[:, 0:n], a[:, 0:n], a[:, (1 << d):(1 << d) + n], ALU.add))
                    a = b
                s = a[:, 8 - half:8 - half + L]
                link(eng.tensor_tensor(s[:, 0:8], s[:, 0:8], edge[:, 16 * g:16 * g + 8], ALU.mult))
                link(eng.tensor_tensor(s[:, L - 8:L], s[:, L - 8:L], edge[:, 16 * g + 8:16 * g + 16], ALU.mult))
                link(eng.tensor_scalar(s, s, 1.0 / (2 * half), 1.0, ALU.mult, ALU.mult))
                eng.tensor_tensor(x, s, x, ALU.subtract).then_inc(pool_done, 1)
                eng.wait_ge(pool_done, g + 1)

        @block.scalar
        def _(eng):
            for i, (x, n) in enumerate(SQ):
                if i >= 2:
                    eng.wait_ge(sum_mm, i - 1)
                eng.activation(prob(i % 2)[:, 0:n], x, ACT.Square).then_inc(sq_done, 1)
            eng.wait_ge(sum_mm, 4)
            eng.activation(tb, ps[0][:], ACT.Sqrt, bias=eps[:, 0:1], scale=1.0 / 512).then_inc(root_done, 1)
            eng.wait_ge(sum_mm, 6)
            eng.activation(prob(0)[:, 0:L], ps[1][:], ACT.Sqrt, bias=eps[:, 0:1], scale=1.0 / 256)
            eng.activation(prob(0)[:, L:LK], ps[2][:, 0:LC], ACT.Sqrt, bias=eps[:, 0:1], scale=1.0 / 256).then_inc(root_done, 1)
            eng.wait_ge(kr_done, 1)
            eng.activation(kr_hi[:], k_rope, ACT.Copy).then_inc(kr_cut, 1)
            for i in range(4):
                eng.wait_ge(nrm_done, i + 1)
                eng.activation(qn_hi[:, i * L:(i + 1) * L], q_t(i), ACT.Copy).then_inc(nrm_hi, 1)
            for i in range(2):
                eng.wait_ge(nrm_done, 5 + i)
                eng.activation(kv_hi[:, i * LK:(i + 1) * LK], kv_t(i), ACT.Copy).then_inc(nrm_hi, 1)

            def pair(p, early=False, last=False):
                if not early:
                    eng.wait_ge(pv_mm, 2 * p)
                eng.wait_ge(pr_mm, 8 * p + 1)
                eng.activation(ta, ps[2][:], ACT.Copy).then_inc(qr_copy, 1)
                for i in range(2):
                    eng.wait_ge(pr_mm, 8 * p + 2 + i)
                    eng.activation(q_hi[:, i * L:(i + 1) * L], ps[i][:], ACT.Copy).then_inc(pr_hi, 1)
                for i in range(2):
                    eng.wait_ge(pr_mm, 8 * p + 4 + i)
                    eng.activation(k_hi[:, i * LK:(i + 1) * LK].rearrange("p (a b) -> p a b", a=2),
                                   psum[:, 4 + 2 * i:6 + 2 * i, 0:384], ACT.Copy).then_inc(pr_hi, 1)
                eng.wait_ge(qr_rot, p + 1)
                eng.activation(q_hi[:, 2 * L:3 * L], tb, ACT.Copy).then_inc(pr_hi, 1)
                for i in range(3):
                    eng.wait_ge(pr_mm, 8 * p + 6 + i)
                    eng.activation(v_hi[:, i * L:(i + 1) * L], ps[i][:], ACT.Copy).then_inc(pr_hi, 1)

                def exp(n):
                    s = n % 2
                    eng.wait_ge(max_done, 8 * p + n + 1)
                    if not (early and n < 2):
                        eng.wait_ge(t_mm, 8 * p + n - 1)
                    eng.activation(prob(s).rearrange("p (a b) -> p a b", a=2), psum[:, 2 * s:2 * s + 2, 0:384], ACT.Exp,
                                   bias=st[:, 4 * s + 1:4 * s + 2], scale=SCALE, accum_out=st[:, 4 * s + 2:4 * s + 3]).then_inc(e_done, 1)

                def cut(n):
                    eng.wait_ge(t_mm, 8 * p + n + 1)
                    if n == 4:
                        eng.wait_ge(pv_mm, 2 * p + 1)
                    o = (n % 4) * P
                    eng.activation(pt_hi[:].rearrange("p (k q) -> p k q", k=6)[:, :, o:o + P],
                                   psum[:, 4:6, :].rearrange("p a b -> p (a b)")[:, 0:LK].rearrange("p (k q) -> p k q", k=6),
                                   ACT.Copy).then_inc(pt_hi_done, 1)

                for n in range(10):
                    if n >= 2:
                        cut(n - 2)
                    if n < 8:
                        exp(n)
                    if n in (3, 5) and not last:
                        weights(p + 1, n == 5)

            def weights(p, half, early=False):
                a, b = (1280, 2560) if half else (0, 1280)
                if not half:
                    eng.wait_ge(w_in, 16 * p + 16)
                    if not early:
                        eng.wait_ge(pr_mm, 8 * p)
                eng.activation(w_hi[:, a:b], raw[:, a:b], ACT.Copy).then_inc(wh_hi, 1)

            weights(0, False, True)
            weights(0, True, True)
            pair(0, early=True)
            with eng.Fori(1, 3) as p:
                pair(p)
            pair(3, last=True)

        @block.vector
        def _(eng):
            eng.wait_ge(tab_in, 80)
            eng.tensor_tensor(ta, k_rope[:, 0:L], rope_c, ALU.mult).then_inc(step, 1)
            eng.wait_ge(kr_mm, 1)
            eng.wait_ge(step, 1)
            eng.tensor_tensor(k_rope[:, 0:L], ps[3][:], rope_s, ALU.mult).then_inc(step, 1)
            eng.wait_ge(step, 2)
            eng.tensor_tensor(k_rope[:, 0:L], k_rope[:, 0:L], ta, ALU.add).then_inc(kr_done, 1)
            eng.wait_ge(root_done, 1)
            eng.reciprocal(tb, tb).then_inc(rst_done, 1)
            eng.wait_ge(root_done, 2)
            eng.reciprocal(r_kv, prob(0)).then_inc(rst_done, 1)
            eng.wait_ge(kr_done, 1)
            eng.wait_ge(kr_cut, 1)
            eng.tensor_tensor(kr_lo[:], k_rope, kr_hi[:], ALU.subtract).then_inc(kr_cut, 1)
            eng.wait_ge(rst_done, 2)
            for i in range(6):
                x, r, col = (q_t(i), tb, P_QG + i) if i < 4 else (kv_t(i - 4), r_kv, P_KG + i - 4)
                eng.scalar_tensor_tensor(out=x, in0=x, scalar=par[:, col:col + 1], in1=r, op0=ALU.mult, op1=ALU.mult).then_inc(nrm_done, 1)
            for i in range(6):
                eng.wait_ge(nrm_done, i + 1)
                eng.wait_ge(nrm_hi, i + 1)
                hi, lo, x = ((qn_hi[:, i * L:(i + 1) * L], qn_lo[:, i * L:(i + 1) * L], q_t(i)) if i < 4 else
                             (kv_hi[:, (i - 4) * LK:(i - 3) * LK], kv_lo[:, (i - 4) * LK:(i - 3) * LK], kv_t(i - 4)))
                eng.tensor_tensor(lo, x, hi, ALU.subtract).then_inc(nrm_lo, 1)

            def pair(p, early=False, last=False):
                eng.wait_ge(qr_copy, p + 1)
                eng.tensor_tensor(tb, ta, rope_c, ALU.mult).then_inc(step, 1)
                eng.wait_ge(qr_mm, p + 1)
                eng.wait_ge(step, 2 * p + 3)
                eng.tensor_tensor(ta, ps[3][:], rope_s, ALU.mult).then_inc(step, 1)
                eng.wait_ge(step, 2 * p + 4)
                eng.tensor_tensor(tb, tb, ta, ALU.add).then_inc(qr_rot, 1)
                for i in range(2):
                    eng.wait_ge(pr_hi, 8 * p + i + 1)
                    eng.tensor_tensor(q_lo[:, i * L:(i + 1) * L], ps[i][:], q_hi[:, i * L:(i + 1) * L], ALU.subtract).then_inc(pr_lo, 1)
                for i in range(2):
                    eng.wait_ge(pr_hi, 8 * p + i + 3)
                    lo, hi = (z[:, i * LK:(i + 1) * LK].rearrange("p (a b) -> p a b", a=2) for z in (k_lo, k_hi))
                    eng.tensor_tensor(lo, psum[:, 4 + 2 * i:6 + 2 * i, 0:384], hi, ALU.subtract).then_inc(pr_lo, 1)
                eng.wait_ge(pr_hi, 8 * p + 5)
                eng.wait_ge(qr_rot, p + 1)
                eng.tensor_tensor(q_lo[:, 2 * L:3 * L], tb, q_hi[:, 2 * L:3 * L], ALU.subtract).then_inc(pr_lo, 1)
                for i in range(3):
                    eng.wait_ge(pr_hi, 8 * p + 6 + i)
                    eng.tensor_tensor(v_lo[:, i * L:(i + 1) * L], ps[i][:], v_hi[:, i * L:(i + 1) * L], ALU.subtract).then_inc(pr_lo, 1)

                def peak(n):
                    s = n % 2
                    eng.wait_ge(s_mm, 8 * p + n + 1)
                    eng.tensor_reduce(st[:, 4 * s:4 * s + 1], psum[:, 2 * s:2 * s + 2, 0:384], AX.XY, ALU.max).then_inc(st_max, 1)
                    eng.wait_ge(st_max, 8 * p + n + 1)
                    eng.tensor_scalar(st[:, 4 * s + 1:4 * s + 2], st[:, 4 * s:4 * s + 1], -SCALE, None, ALU.mult).then_inc(max_done, 1)

                def norm(n):
                    s = n % 2
                    eng.wait_ge(e_done, 8 * p + n + 1)
                    eng.reciprocal(st[:, 4 * s + 3:4 * s + 4], st[:, 4 * s + 2:4 * s + 3]).then_inc(st_rec, 1)
                    eng.wait_ge(st_rec, 8 * p + n + 1)
                    eng.tensor_scalar(prob(s), prob(s), st[:, 4 * s + 3:4 * s + 4], None, ALU.mult).then_inc(p_done, 1)

                def cut(n):
                    eng.wait_ge(pt_hi_done, 8 * p + n + 1)
                    o = (n % 4) * P
                    lo, hi = (z[:].rearrange("p (k q) -> p k q", k=6)[:, :, o:o + P] for z in (pt_lo, pt_hi))
                    eng.tensor_tensor(lo, psum[:, 4:6, :].rearrange("p a b -> p (a b)")[:, 0:LK].rearrange("p (k q) -> p k q", k=6),
                                      hi, ALU.subtract).then_inc(pt_lo_done, 1)

                def gate(hh):
                    eng.wait_ge(pv_mm, 2 * p + hh + 1)
                    g = UG[:, bass.ds((4 + 2 * p + hh) * L, L)]
                    eng.tensor_tensor(g, ps[6 + hh][:], g, ALU.mult).then_inc(o_done, 1)

                for n in range(10):
                    if n < 8:
                        peak(n)
                    if 1 <= n < 9:
                        norm(n - 1)
                    if n >= 2:
                        cut(n - 2)
                    if n in (4, 6) and not last:
                        weights(p + 1, n == 6)
                    if n == 7:
                        gate(0)
                gate(1)

            def weights(p, half):
                a, b = (1280, 2560) if half else (0, 1280)
                eng.wait_ge(wh_hi, 2 * p + (2 if half else 1))
                eng.tensor_tensor(w_lo[:, a:b], raw[:, a:b], w_hi[:, a:b], ALU.subtract).then_inc(wh_lo, 1)

            weights(0, False)
            weights(0, True)
            pair(0, early=True)
            with eng.Fori(1, 3) as p:
                pair(p)
            pair(3, last=True)
            for g in range(4):
                eng.wait_ge(pool_mm, g + 1)
                x = UG[:, (12 + g) * L:(13 + g) * L]
                eng.scalar_tensor_tensor(out=x, in0=ps[g][:], scalar=par[:, P_PS + g:P_PS + g + 1], in1=x,
                                         op0=ALU.mult, op1=ALU.mult).then_inc(pool_out, 1)

        @block.tensor
        def _(eng):
            def passes(dst, ws, xs, first, last):
                for m, (w, x) in enumerate(((ws[0], xs[0]), (ws[0], xs[1]), (ws[1], xs[0]))):
                    mm = eng.matmul(dst, w, x, start=first and m == 0, stop=last and m == 2)
                return mm

            def both(hi, lo, a, n, rows=slice(None)):
                return hi[rows, a:a + n], lo[rows, a:a + n]

            eng.wait_ge(tab_in, 80)
            eng.matmul(ps[3][:], swap[:], k_rope[:, 0:L], start=True, stop=True).then_inc(kr_mm, 1)
            for i in range(6):
                eng.wait_ge(sq_done, i + 1)
                x = prob(i % 2)
                if i < 4:
                    eng.matmul(ps[0][:], ones[:], x[:, 0:L], start=(i == 0), stop=(i == 3)).then_inc(sum_mm, 1)
                else:
                    eng.matmul(ps[1][:], ones[:], x[:, 0:L], start=(i == 4), stop=(i == 5))
                    eng.matmul(ps[2][:, 0:LC], ones[:], x[:, L:LK], start=(i == 4), stop=(i == 5)).then_inc(sum_mm, 1)
            eng.wait_ge(nrm_lo, 6)
            eng.wait_ge(kr_cut, 2)
            eng.wait_ge(root_done, 2)

            def pair(p, early=False, last=False):
                eng.wait_ge(wh_lo, 2 * p + 2)
                if not early:
                    eng.wait_ge(max_done, 8 * p)
                    eng.wait_ge(e_done, 8 * p)
                    eng.wait_ge(o_done, 2 * p)
                for dst, off in ((2, 2 * P), (0, 0), (1, P)):
                    for k in range(4):
                        a = k * 384 + off
                        mm = passes(ps[dst][:], both(w_hi, w_lo, a, P), both(qn_hi, qn_lo, k * L, L), k == 0, k == 3)
                    mm.then_inc(pr_mm, 1)
                eng.wait_ge(qr_copy, p + 1)
                eng.matmul(ps[3][:], swap[:], ta, start=True, stop=True).then_inc(qr_mm, 1)
                if not early:
                    eng.wait_ge(pt_lo_done, 8 * p)
                for hh in range(2):
                    for half in range(2):
                        for k in range(2):
                            a = 4 * 384 + k * 512 + hh * P
                            mm = passes(psum[:, 4 + 2 * hh + half, 0:384], both(w_hi, w_lo, a, P),
                                        both(kv_hi, kv_lo, k * LK + half * 384, 384), k == 0, k == 1)
                    mm.then_inc(pr_mm, 1)
                for b in range(3):
                    if b < 2:
                        eng.wait_ge(pr_lo, 8 * p + 1 + b)
                    for i in range(2):
                        for k in range(2):
                            a = 4 * 384 + k * 512 + 256
                            mm = passes(ps[b][:, i * 256:(i + 1) * 256], both(kv_hi, kv_lo, k * LK + (2 * b + i) * P, P),
                                        both(w_hi, w_lo, a, 256), k == 0, k == 1)
                    mm.then_inc(pr_mm, 1)
                eng.wait_ge(pr_lo, 8 * p + 8)
                eng.wait_ge(step, 2 * p + 4)

                def scores(n):
                    hh, qt, s = n // 4, n % 4, n % 2
                    if n >= 2:
                        eng.wait_ge(e_done, 8 * p + n - 1)
                    rows = slice(64 * hh, 64 * hh + 64)
                    for half in range(2):
                        passes(psum[:, 2 * s + half, 0:384], both(q_hi, q_lo, hh * L + qt * P, P),
                               both(k_hi, k_lo, hh * LK + half * 384, 384), True, False)
                        mm = passes(psum[:, 2 * s + half, 0:384], both(q_hi, q_lo, 2 * L + qt * P, P, rows),
                                    both(kr_hi, kr_lo, half * 384, 384, rows), False, True)
                    mm.then_inc(s_mm, 1)

                def turn(n):
                    eng.wait_ge(p_done, 8 * p + n + 1)
                    if n >= 1:
                        eng.wait_ge(pt_lo_done, 8 * p + n)
                    for k in range(6):
                        mm = eng.transpose(psum[:, 4 + k // 4, (k % 4) * P:(k % 4 + 1) * P],
                                           prob(n % 2)[:, k * P:(k + 1) * P], ident[:])
                    mm.then_inc(t_mm, 1)

                def values(hh):
                    eng.wait_ge(pt_lo_done, 8 * p + 4 * hh + 4)
                    for k in range(6):
                        mm = passes(ps[6 + hh][:], both(v_hi, v_lo, k * 256 + hh * P, P), both(pt_hi, pt_lo, k * L, L), k == 0, k == 5)
                    mm.then_inc(pv_mm, 1)

                for n in range(10):
                    if n < 8:
                        scores(n)
                    if n == 6:
                        values(0)
                    if n >= 2:
                        turn(n - 2)
                values(1)

            pair(0, early=True)
            with eng.Fori(1, 3) as p:
                pair(p)
            pair(3, last=True)
            eng.wait_ge(e_done, 32)
            for g in range(4):
                eng.wait_ge(pool_done, g + 1)
                eng.matmul(ps[g][:], wp[:, g * P:(g + 1) * P], U[:, (T_POOL + g) * L:(T_POOL + g + 1) * L],
                           start=True, stop=True).then_inc(pool_mm, 1)


def emit(nc, mem, t, out):
    gcol, UG, ident, ones, eps = (mem[n] for n in ("gcol", "UG", "ident", "ones", "eps"))
    with ExitStack() as ctx:
        def alloc(name, cols, dt=F32):
            return ctx.enter_context(nc.sbuf_tensor(name, [P, cols], dt))

        def sem(name):
            return ctx.enter_context(nc.semaphore(name))

        m_hi, m_lo = alloc("m_hi", KT * L, F32R), alloc("m_lo", KT * L, F32R)
        raw = alloc("wo_raw", 2 * 2048)
        w_hi, w_lo = alloc("wo_hi", 2 * 2048, F32R), alloc("wo_lo", 2 * 2048, F32R)
        gate = alloc("gate_rows", D)
        gain = UG[:, 6144:8192]
        y = alloc("y", 4 * D)
        tmp = alloc("out_tmp", L)
        ss, rs = alloc("row_sums", 16), alloc("row_scale", 8)
        psum = ctx.enter_context(nc.psum_tensor("po", [P, 8, 512], F32))

        x_in, gain_in = sem("x_rows_in"), sem("gain_in")
        w_in = [sem(f"wo_in{s}") for s in range(2)]
        mix_hi, mix_lo, diag_done, gate_mm, gate_out = sem("mix_hi"), sem("mix_lo"), sem("diag_done"), sem("gate_rows_mm"), sem("gate_out")
        wo_hi, wo_lo, wo_mm, mm_done = sem("wo_hi_done"), sem("wo_lo_done"), sem("wo_mm"), sem("wo_bank_mm")
        scaled, y_done, sq_done, root_done, fin_done, stored = (sem("out_scaled"), sem("y_done_o"), sem("sq_done_o"), sem("root_done_o"),
                                                                sem("fin_done"), sem("stored"))
        row_sum, row_scale = sem("row_sum"), sem("row_scale_done")
        block = ctx.enter_context(nc.Block())

        @block.sync
        def _(eng):
            for n in range(16):
                s = n % 2
                if n >= 2:
                    eng.wait_ge(wo_lo, n - 1)
                eng.dma_start(raw[:, s * 2048:(s + 1) * 2048], t["w_out"][n, :, :]).then_inc(w_in[s], 16)
                if n == 1:
                    for i in range(4):
                        eng.dma_start(y[:, i * D:(i + 1) * D], t["x"][i * P:(i + 1) * P, :]).then_inc(x_in, 16)
                if n == 4:
                    eng.wait_ge(mix_lo, 16)
                    eng.dma_start(gain, t["gain"].to_broadcast([P, D])).then_inc(gain_in, 16)
            for i in range(4):
                eng.wait_ge(fin_done, i + 1)
                eng.dma_start(out[i * P:(i + 1) * P, :], y[:, i * D:(i + 1) * D]).then_inc(stored, 16)
            eng.wait_ge(stored, 64)

        @block.scalar
        def _(eng):
            def mixed(i):
                eng.activation(m_hi[:, i * L:(i + 1) * L], UG[:, i * L:(i + 1) * L], ACT.Copy).then_inc(mix_hi, 1)

            def high(n):
                s = n % 2
                eng.wait_ge(w_in[s], 16 * (n // 2) + 16)
                if n >= 2:
                    b, c = (n - 2) // 4, (n - 2) % 4
                    eng.wait_ge(mm_done if c == 3 else wo_mm, 4 * b + 4 if c == 3 else 3 * b + c + 1)
                eng.activation(w_hi[:, s * 2048:(s + 1) * 2048], raw[:, s * 2048:(s + 1) * 2048], ACT.Copy).then_inc(wo_hi, 1)

            def squares(b, tok):
                n = 4 * b + tok
                eng.wait_ge(y_done, n + 1)
                if n:
                    eng.wait_ge(sq_done, n)
                eng.activation(tmp[:], y[:, tok * D + b * L:tok * D + (b + 1) * L], ACT.Square,
                               accum_out=ss[:, 4 * tok + b:4 * tok + b + 1]).then_inc(sq_done, 1)

            for i in range(4):
                mixed(i)
            high(0)
            for i in range(4, 8):
                mixed(i)
            high(1)
            for i in range(8, 16):
                mixed(i)
            for n in range(2, 16):
                high(n)
                if n % 4 == 1 and n > 4:
                    for tok in range(4):
                        squares(n // 4 - 1, tok)
            for tok in range(4):
                squares(3, tok)
                eng.wait_ge(row_sum, tok + 1)
                eng.activation(rs[:, 2 * tok:2 * tok + 1], rs[:, 2 * tok:2 * tok + 1], ACT.Sqrt, bias=eps[:, 0:1], scale=1.0 / D).then_inc(root_done, 1)

        @block.vector
        def _(eng):
            def mixed(i):
                eng.wait_ge(mix_hi, i + 1)
                eng.tensor_tensor(m_lo[:, i * L:(i + 1) * L], UG[:, i * L:(i + 1) * L], m_hi[:, i * L:(i + 1) * L], ALU.subtract).then_inc(mix_lo, 1)

            def low(n):
                s = n % 2
                eng.wait_ge(wo_hi, n + 1)
                eng.tensor_tensor(w_lo[:, s * 2048:(s + 1) * 2048], raw[:, s * 2048:(s + 1) * 2048],
                                  w_hi[:, s * 2048:(s + 1) * 2048], ALU.subtract).then_inc(wo_lo, 1)

            for i in range(16):
                if i >= 4:
                    eng.wait_ge(gate_mm, i - 3)
                eng.tensor_scalar(tmp[:, (i % 4) * P:(i % 4 + 1) * P], ident[:], gcol[:, i:i + 1], None, ALU.mult).then_inc(diag_done, 1)
            for i in range(4):
                mixed(i)
            low(0)
            for i in range(4, 8):
                mixed(i)
            low(1)
            for i in range(8, 16):
                mixed(i)
            eng.wait_ge(gate_mm, 16)
            eng.tensor_copy(gate[:].rearrange("p (a b) -> p a b", a=4), psum[:, 4:8, :]).then_inc(gate_out, 1)
            eng.wait_ge(gate_out, 1)
            eng.wait_ge(x_in, 64)

            def residual(b, tok):
                n = 4 * b + tok
                eng.wait_ge(mm_done, n + 1)
                yy = y[:, tok * D + b * L:tok * D + (b + 1) * L]
                bank = psum[:, 4 * (b % 2) + tok, :]
                eng.tensor_tensor(bank, bank, gate[:, b * L:(b + 1) * L], ALU.mult).then_inc(scaled, 1)
                eng.wait_ge(scaled, n + 1)
                eng.tensor_tensor(yy, bank, yy, ALU.add).then_inc(y_done, 1)

            for n in range(2, 16):
                low(n)
                if n % 4 == 1 and n > 4:
                    for tok in range(4):
                        residual(n // 4 - 1, tok)
            eng.wait_ge(gain_in, 16)
            for tok in range(4):
                residual(3, tok)
                eng.wait_ge(sq_done, 13 + tok)
                r = rs[:, 2 * tok:2 * tok + 2]
                eng.tensor_reduce(r[:, 0:1], ss[:, 4 * tok:4 * tok + 4], AX.X, ALU.add).then_inc(row_sum, 1)
                eng.wait_ge(root_done, tok + 1)
                eng.reciprocal(r[:, 1:2], r[:, 0:1]).then_inc(row_scale, 1)
                eng.wait_ge(row_scale, tok + 1)
                yy = y[:, tok * D:(tok + 1) * D]
                eng.scalar_tensor_tensor(out=yy, in0=yy, scalar=r[:, 1:2], in1=gain, op0=ALU.mult, op1=ALU.mult).then_inc(fin_done, 1)

        @block.tensor
        def _(eng):
            for i in range(16):
                eng.wait_ge(diag_done, i + 1)
                eng.matmul(psum[:, 4 + i // 4, (i % 4) * P:(i % 4 + 1) * P], ones[:], tmp[:, (i % 4) * P:(i % 4 + 1) * P],
                           start=True, stop=True).then_inc(gate_mm, 1)
            for b in range(4):
                if b == 1:
                    eng.wait_ge(gate_out, 1)
                if b >= 2:
                    eng.wait_ge(y_done, 4 * (b - 1))
                for c in range(4):
                    n = 4 * b + c
                    s = n % 2
                    eng.wait_ge(wo_lo, n + 1)
                    for tok in range(4):
                        for k in range(4):
                            kk = 4 * c + k
                            if b == 0 and tok == 0:
                                eng.wait_ge(mix_lo, kk + 1)
                            x, w = kk * L + tok * P, s * 2048 + k * L
                            for m, (a, v) in enumerate(((m_hi, w_hi), (m_hi, w_lo), (m_lo, w_hi))):
                                mm = eng.matmul(psum[:, 4 * (b % 2) + tok, :], a[:, x:x + P], v[:, w:w + L],
                                                start=(kk == 0 and m == 0), stop=(kk == 15 and m == 2))
                        if c == 3:
                            mm.then_inc(mm_done, 1)
                    if c < 3:
                        mm.then_inc(wo_mm, 1)


OUT, RET = [L, D], (1, L, D)


def build(nc, t, out):
    with ExitStack() as ctx:
        def alloc(name, cols):
            return ctx.enter_context(nc.sbuf_tensor(name, [P, cols], F32))

        mem = {n: alloc(n, c) for n, c in (("par", N_PAR), ("gcol", 16), ("ident", P), ("ones", P), ("eps", 1), ("UG", KT * L))}
        with nc.sbuf_tensor("U", [P, U_COLS], F32) as U:
            mem["U"] = U
            project(nc, mem, t)
            hyena(nc, mem, t)
            attend(nc, mem, t)
        emit(nc, mem, t, out)


def layout(inputs):
    f = {n: np.asarray(a) for n, a in inputs.items()}

    def cols(a, n):
        return np.ascontiguousarray(a.reshape(n, P).T)

    w_ada, b_ada, w_in = f["w_ada"][0], f["b_ada"][0], f["w_in"][0]
    par = np.concatenate([
        cols(b_ada[:D], 16), cols(b_ada[D:2 * D], 16), cols(b_ada[2 * D:], 16), cols(f["norm_g"][0], 16),
        cols(f["hy_conv_w"][0], 36), cols(f["hy_conv_b"][0], 12), cols(f["hy_bias"][0], 8),
        cols(f["q_norm_g"][0], 4), cols(f["kv_norm_g"][0], 2), cols(f["pool_scale"][0], 4)], axis=1)
    o_hg, o_q, o_kv, o_kr, o_mg, o_pool, o_pg = 1536, 2048, 2560, 2816, 2880, 3904, 4416

    def tile(o):
        return w_in[:, o:o + P]

    k_rope = w_in[:, o_kr:o_kr + DR]
    first = [tile(0), tile(P), tile(o_kv), tile(o_kv + P), np.concatenate([k_rope, k_rope], axis=1)]
    rest = ([tile(i * P) for i in range(2, 12)] + [tile(o_pool + i * P) for i in range(4)]
            + [tile(o_q + i * P) for i in range(4)] + [tile(o_hg + i * P) for i in range(4)]
            + [tile(o_mg + i * P) for i in range(8)] + [tile(o_pg + i * P) for i in range(4)])
    wa = np.concatenate(first, axis=1).reshape(KT, P, A_TILES * P)
    wb = np.concatenate(rest, axis=1).reshape(CH, CH, P, B_GROUPS, 256).transpose(3, 0, 2, 1, 4)
    ss = np.stack([w_ada[:, :D].reshape(KT, P, KT, P), w_ada[:, D:2 * D].reshape(KT, P, KT, P)], axis=3)
    gate = w_ada[:, 2 * D:].reshape(4, 4, P, 8, 256).transpose(3, 0, 2, 1, 4)
    w = np.pi * (2 * np.arange(HF) + 1) / (2.0 * L)
    waves = [fn(np.outer(2 * np.arange(HF) + odd, w)) for fn in (np.cos, np.sin) for odd in (0, 1)]
    tables = np.concatenate([m[i * P:(i + 1) * P] for m in waves for i in range(2)]
                            + [m.T[i * P:(i + 1) * P] for m in waves for i in range(2)], axis=1)
    f32 = np.float32
    order = np.concatenate([np.arange(0, L, 2), np.arange(1, L, 2)])
    tt = np.linspace(0.0, 1.0, L, dtype=f32)[:, None]
    wpos = f32(2.0 * math.pi / L) * np.arange(L, dtype=f32)[:, None]
    bands = np.linspace(1e-4, 15, 16, dtype=f32)[None, :]
    feats = np.concatenate([tt, np.cos(bands * wpos), -np.sin(bands * wpos)], axis=1).astype(f32)[order]
    deltas = np.abs(np.linspace(math.log(1e-2) / 1.5, math.log(1e-2) / 0.3, L, dtype=f32))
    decay = np.exp(-tt * deltas).astype(f32)[order].reshape(4, P, L)
    back = decay[0].copy()
    back[0] = 0.0
    hf = np.zeros((64, 131), f32)
    hf[0:33, 0:64], hf[:, 64:128] = f["hf_w1"][0], f["hf_w2"][0]
    hf[:, 128], hf[:, 129], hf[:, 130] = f["hf_b1"][0], f["hf_freq"][0], f["hf_b2"][0]
    inv = (f32(10000.0) ** (-np.arange(16, dtype=f32) / f32(16))).astype(f32)
    pos = np.arange(L)
    ang = np.concatenate([(pos // 64).astype(f32)[:, None] * inv, (pos % 64).astype(f32)[:, None] * inv], axis=1)
    ang = np.tile(np.repeat(ang.T, 2, axis=0), (2, 1))
    swap = np.zeros((P, P), f32)
    swap[np.arange(1, P, 2), np.arange(0, P, 2)] = -1.0
    swap[np.arange(0, P, 2), np.arange(1, P, 2)] = 1.0
    edge = np.ones((4, 16), f32)
    for g in range(4):
        h = 1 << g
        at = np.concatenate([np.arange(8), np.arange(L - 8, L)])
        edge[g] = 2 * h / (np.minimum(at + h, L) - np.maximum(at - h, 0))
    uq = f["w_uq"][0].reshape(4, P, 4, 2, DN + DR)
    uq = np.concatenate([uq[..., 0, :DN], uq[..., 1, :DN], uq[..., 0, DN:], uq[..., 1, DN:]], axis=-1)
    ukv = f["w_ukv"][0].reshape(2, P, 4, 2, DN + DV)
    ukv = np.concatenate([ukv[..., 0, :DN], ukv[..., 1, :DN], ukv[..., 0, DN:], ukv[..., 1, DN:]], axis=-1)
    w_heads = np.concatenate([uq.transpose(2, 1, 0, 3).reshape(4, P, 1536), ukv.transpose(2, 1, 0, 3).reshape(4, P, 1024)], axis=2)
    return {
        "rope_c": np.cos(ang).astype(f32), "rope_s": np.sin(ang).astype(f32), "swap": swap,
        "comb": np.array([[1, 0], [0, 1], [1, 0], [0, 1]], f32),
        "edge": np.tile(edge.reshape(1, 64), (P, 1)),
        "w_pool": np.ascontiguousarray(f["w_pool"][0].transpose(1, 0, 2)).reshape(P, 4 * P),
        "w_heads": np.ascontiguousarray(w_heads),
        "x": np.ascontiguousarray(f["x"][0]), "gain": f["final_norm_g"].reshape(1, D),
        "w_out": np.ascontiguousarray(f["w_out"][0].reshape(4, 4, P, 4, L).transpose(3, 0, 2, 1, 4)).reshape(16, P, 4 * L),
        "tables": tables.astype(f32),
        "feats": np.ascontiguousarray(feats.T),
        "decay": np.ascontiguousarray(np.concatenate([*decay, back], axis=1)),
        "hf": hf,
        "w3": np.ascontiguousarray(f["hf_w3"][0].reshape(64, 2, 1024).transpose(1, 0, 2)),
        "ident": np.eye(P, dtype=f32),
        "cond": np.stack([cols(f["c"], KT), cols(f["c_ctx"], KT)], axis=2).reshape(P, 2 * KT),
        "par": par,
        "xT": np.ascontiguousarray(f["x"][0].T.reshape(KT, P, L).transpose(1, 0, 2)).reshape(P, KT * L),
        "cT": np.ascontiguousarray(f["ctx"][0].T.reshape(KT, P, LC).transpose(1, 0, 2)).reshape(P, KT * LC),
        "w_ada": np.ascontiguousarray(ss.transpose(2, 1, 0, 3, 4)).reshape(KT, P, 4096),
        "w_gate": np.ascontiguousarray(gate).reshape(32, P, 1024),
        "wa": np.ascontiguousarray(wa),
        "wb": np.ascontiguousarray(wb).reshape(4 * B_GROUPS, P, CH * 256),
    }


def kernel(**inputs):
    import concourse.bacc as _bacc
    from concourse.bass_utils import run_bass_kernel_spmd as _run

    arrays = layout(inputs)
    nc = _bacc.Bacc("TRN2", target_bir_lowering=False, num_devices=1)
    t = {n: nc.dram_tensor(f"in_{n}_dram", a.shape, mybir.dt.from_np(a.dtype), kind="ExternalInput").ap()
         for n, a in arrays.items()}
    out = nc.dram_tensor("out_dram", OUT, F32, kind="ExternalOutput").ap()
    build(nc, t, out)
    r = _run(nc, [{f"in_{n}_dram": a for n, a in arrays.items()}], core_ids=[0])
    return r.results[0]["out_dram"].reshape(RET)
```
